# Optimizing a Trainium2 kernel written in Bass

```python
import math
import jax, jax.numpy as jnp
from jax import lax
import numpy as np

D_MODEL = 1024
BATCH = 1
SEQ = 1024
DEPTH = 2
DEC_BATCH = 8
DEC_SEQ = 16
PAST_LEN = 256

CHUNK = 64
N_MIXERS = 2
N_S5_LAYERS = (DEPTH + 1) // 2
N_MLSTM_LAYERS = DEPTH // 2
S5_GROUP_CH = 16
S5_GROUPS = D_MODEL // S5_GROUP_CH
S5_STATE = 64
MLSTM_PROJ = 2
MLSTM_INNER = MLSTM_PROJ * D_MODEL
MLSTM_HEADS = 4
MLSTM_HEAD_DIM = MLSTM_INNER // MLSTM_HEADS
MLSTM_CONV = 4
QKV_BLOCK = 4
N_QKV_BLOCKS = MLSTM_INNER // QKV_BLOCK
D_FF = 2816
FFN_CONV = 3
NORM_EPS = 1e-6
LN_EPS = 1e-5
F_BIAS_LO = 3.0
F_BIAS_HI = 6.0

kernel_name = "s5_mlstm_interleaved_streaming_step"

def rms_norm(x, g):
    xf = x.astype(jnp.float32)
    y = xf * lax.rsqrt(jnp.mean(xf * xf, axis=-1, keepdims=True) + NORM_EPS)
    return (y * g.astype(jnp.float32)).astype(x.dtype)

def causal_dwconv(x, buf, w, b):
    width = w.shape[0]
    s = x.shape[1]
    xp = jnp.concatenate([buf.astype(x.dtype), x], axis=1)
    y = b + xp[:, 0:s] * w[0]
    for j in range(1, width):
        y = y + xp[:, j:j + s] * w[j]
    return y, xp[:, xp.shape[1] - (width - 1):]

def s5_mixer(u, h_re, h_im, A_re, A_im, log_dt, B_re, B_im, C_re, C_im, d_skip, w_glu):
    f32 = jnp.float32
    bsz, s, _ = u.shape
    L = min(CHUNK, s)
    nc = s // L
    A = lax.complex(A_re.astype(f32), A_im.astype(f32))
    dt = jnp.exp(log_dt.astype(f32))[:, None]
    A_bar = jnp.exp(A * dt)
    B_bar = ((A_bar - 1.0) / A)[..., None] * lax.complex(B_re.astype(f32), B_im.astype(f32))
    C_mat = lax.complex(C_re.astype(f32), C_im.astype(f32))
    u_chunks = jnp.moveaxis(u.astype(f32).reshape(bsz, nc, L, S5_GROUPS, S5_GROUP_CH), 1, 0)

    def combine(e1, e2):
        a1, b1 = e1
        a2, b2 = e2
        return a1 * a2, a2 * b1 + b2

    def step(h, uc):
        bu = jnp.einsum('gnc,blgc->blgn', B_bar, uc.astype(jnp.complex64))
        bu = bu.at[:, 0].add(A_bar * h)
        a = jnp.broadcast_to(A_bar, bu.shape)
        _, hs = lax.associative_scan(combine, (a, bu), axis=1)
        y = jnp.einsum('gcn,blgn->blgc', C_mat, hs).real
        return hs[:, -1], y

    h0 = lax.complex(h_re.astype(f32), h_im.astype(f32))
    hT, y = lax.scan(step, h0, u_chunks)
    y = jnp.moveaxis(y, 0, 1).reshape(bsz, s, D_MODEL) + d_skip.astype(f32) * u.astype(f32)
    z = jax.nn.gelu(y, approximate=True).astype(u.dtype)
    ag = z @ w_glu
    out = ag[..., :D_MODEL] * jax.nn.sigmoid(ag[..., D_MODEL:])
    return out, hT.real, hT.imag

def headwise(x, w):
    xb = x.reshape(x.shape[:-1] + (N_QKV_BLOCKS, QKV_BLOCK))
    return jnp.einsum('bsnc,ncd->bsnd', xb, w).reshape(x.shape)

def mlstm_chunkwise(q, k, v, i_pre, log_f, C0, n0, m0):
    bsz, s, nh, dh = q.shape
    L = min(CHUNK, s)
    nc = s // L
    causal = jnp.tril(jnp.ones((L, L), dtype=bool))

    def to_chunks(t):
        return jnp.moveaxis(t.reshape((bsz, nc, L) + t.shape[2:]), 1, 0)

    def step(carry, xs):
        C, n, m = carry
        qc, kc, vc, ic, fc = xs
        b = jnp.cumsum(fc, axis=1)
        inter = b + m[:, None, :]
        dmat = b[:, :, None, :] - b[:, None, :, :] + ic[:, None, :, :]
        dmat = jnp.where(causal[None, :, :, None], dmat, -jnp.inf)
        m_t = jnp.maximum(inter, jnp.max(dmat, axis=2))
        wts = jnp.exp(dmat - m_t[:, :, None, :])
        sc = jnp.einsum('bqhd,bshd->bqsh', qc, kc) * wts
        a = jnp.exp(inter - m_t)
        num = jnp.einsum('bqsh,bshd->bqhd', sc, vc) + a[..., None] * jnp.einsum('bqhk,bhvk->bqhv', qc, C)
        den = jnp.sum(sc, axis=2) + a * jnp.einsum('bqhk,bhk->bqh', qc, n)
        h = num / jnp.maximum(jnp.abs(den), jnp.exp(-m_t))[..., None]
        bL = b[:, -1, :]
        g = bL[:, None, :] - b + ic
        m_new = jnp.maximum(bL + m, jnp.max(g, axis=1))
        decay = jnp.exp(bL + m - m_new)
        wg = jnp.exp(g - m_new[:, None, :])
        C_new = decay[..., None, None] * C + jnp.einsum('blh,blhv,blhk->bhvk', wg, vc, kc)
        n_new = decay[..., None] * n + jnp.einsum('blh,blhk->bhk', wg, kc)
        return (C_new, n_new, m_new), h

    xs = (to_chunks(q), to_chunks(k), to_chunks(v), to_chunks(i_pre), to_chunks(log_f))
    (C, n, m), h = lax.scan(step, (C0, n0, m0), xs)
    h = jnp.moveaxis(h, 0, 1).reshape(bsz, s, nh, dh)
    return h, C, n, m

def mlstm_mixer(x, C0, n0, m0, conv_buf, w_up, conv_w, conv_b, wq, wk, wv, w_gate, b_gate, norm_g, skip, w_down):
    f32 = jnp.float32
    bsz, s, _ = x.shape
    up = x @ w_up
    xm, z = up[..., :MLSTM_INNER], up[..., MLSTM_INNER:]
    xc_pre, new_buf = causal_dwconv(xm, conv_buf, conv_w, conv_b)
    xc = jax.nn.silu(xc_pre)
    q = headwise(xc, wq)
    k = headwise(xc, wk)
    v = headwise(xm, wv)
    gates = (q @ w_gate[:MLSTM_INNER] + k @ w_gate[MLSTM_INNER:2 * MLSTM_INNER]
             + v @ w_gate[2 * MLSTM_INNER:]).astype(f32) + b_gate.astype(f32)
    i_pre = gates[..., :MLSTM_HEADS]
    log_f = jax.nn.log_sigmoid(gates[..., MLSTM_HEADS:])

    def heads(t):
        return t.astype(f32).reshape(bsz, s, MLSTM_HEADS, MLSTM_HEAD_DIM)

    h, C, n, m = mlstm_chunkwise(heads(q), heads(k) * (MLSTM_HEAD_DIM ** -0.5), heads(v), i_pre, log_f,
                                 C0.astype(f32), n0.astype(f32), m0.astype(f32))
    mu = jnp.mean(h, axis=-1, keepdims=True)
    var = jnp.mean(jnp.square(h - mu), axis=-1, keepdims=True)
    hn = ((h - mu) * lax.rsqrt(var + LN_EPS)).reshape(bsz, s, MLSTM_INNER) * norm_g.astype(f32)
    hs = hn.astype(x.dtype) + skip * xc
    out = (hs * jax.nn.silu(z)) @ w_down
    return out, C, n, m, new_buf

def conv_ffn(x, buf, w_up, conv_w, conv_b, w_down):
    u = x @ w_up
    uc, new_buf = causal_dwconv(u, buf, conv_w, conv_b)
    gate, val = uc[..., :D_FF], uc[..., D_FF:]
    return (jax.nn.gelu(gate, approximate=True) * val) @ w_down, new_buf

def run_trunk(x, s5_re, s5_im, m_C, m_n, m_m, m_conv, f_conv, w):
    o_re, o_im, o_C, o_n, o_m, o_mconv, o_fconv = [], [], [], [], [], [], []
    for layer in range(DEPTH):
        g = w['norm_g'][layer]
        j = layer // N_MIXERS
        h = rms_norm(x, g[0])
        if layer % N_MIXERS == 0:
            mix, hr, hi = s5_mixer(h, s5_re[j], s5_im[j], w['s5_A_re'][j], w['s5_A_im'][j], w['s5_log_dt'][j],
                                   w['s5_B_re'][j], w['s5_B_im'][j], w['s5_C_re'][j], w['s5_C_im'][j],
                                   w['s5_D'][j], w['s5_w_glu'][j])
            o_re.append(hr)
            o_im.append(hi)
        else:
            mix, C, n, m, cb = mlstm_mixer(h, m_C[j], m_n[j], m_m[j], m_conv[j], w['mlstm_w_up'][j],
                                           w['mlstm_conv_w'][j], w['mlstm_conv_b'][j], w['mlstm_wq'][j],
                                           w['mlstm_wk'][j], w['mlstm_wv'][j], w['mlstm_w_gate'][j],
                                           w['mlstm_b_gate'][j], w['mlstm_norm_g'][j], w['mlstm_skip'][j],
                                           w['mlstm_w_down'][j])
            o_C.append(C)
            o_n.append(n)
            o_m.append(m)
            o_mconv.append(cb)
        x = x + rms_norm(mix, g[1])
        f, fb = conv_ffn(rms_norm(x, g[2]), f_conv[layer], w['ffn_w_up'][layer], w['ffn_conv_w'][layer],
                         w['ffn_conv_b'][layer], w['ffn_w_down'][layer])
        o_fconv.append(fb)
        x = x + rms_norm(f, g[3])
    st = lambda t: jnp.stack(t, axis=0)
    return x, st(o_re), st(o_im), st(o_C), st(o_n), st(o_m), st(o_mconv), st(o_fconv)

def setup_inputs(seed: int = 0) -> dict:
    key = jax.random.key(seed)
    ks = jax.random.split(key, 40)
    f32 = jnp.float32

    def nrm(k, shape, scale):
        return jax.random.normal(k, shape, f32) * scale

    NA, NB = N_S5_LAYERS, N_MLSTM_LAYERS
    a_im_base = jnp.pi * jnp.arange(S5_STATE, dtype=f32)
    b_gate = jnp.concatenate([
        nrm(ks[30], (NB, MLSTM_HEADS), 0.1),
        jnp.linspace(F_BIAS_LO, F_BIAS_HI, MLSTM_HEADS, dtype=f32)[None, :] + nrm(ks[31], (NB, MLSTM_HEADS), 0.01),
    ], axis=-1)
    return {
        'x_prompt': nrm(ks[0], (BATCH, SEQ, D_MODEL), 1.0),
        'x_sample': nrm(ks[1], (DEC_BATCH, DEC_SEQ, D_MODEL), 1.0),
        'state_s5_re': nrm(ks[2], (NA, DEC_BATCH, S5_GROUPS, S5_STATE), 0.1),
        'state_s5_im': nrm(ks[3], (NA, DEC_BATCH, S5_GROUPS, S5_STATE), 0.1),
        'state_mlstm_C': nrm(ks[4], (NB, DEC_BATCH, MLSTM_HEADS, MLSTM_HEAD_DIM, MLSTM_HEAD_DIM), 0.1),
        'state_mlstm_n': nrm(ks[5], (NB, DEC_BATCH, MLSTM_HEADS, MLSTM_HEAD_DIM), 0.1),
        'state_mlstm_m': nrm(ks[6], (NB, DEC_BATCH, MLSTM_HEADS), 1.0),
        'state_mlstm_conv': nrm(ks[7], (NB, DEC_BATCH, MLSTM_CONV - 1, MLSTM_INNER), 1.0),
        'state_ffn_conv': nrm(ks[8], (DEPTH, DEC_BATCH, FFN_CONV - 1, 2 * D_FF), 1.0),
        'norm_g': 1.0 + nrm(ks[9], (DEPTH, 4, D_MODEL), 0.05),
        's5_A_re': -0.5 + nrm(ks[10], (NA, S5_GROUPS, S5_STATE), 0.01),
        's5_A_im': a_im_base + nrm(ks[11], (NA, S5_GROUPS, S5_STATE), 0.01),
        's5_log_dt': jax.random.uniform(ks[12], (NA, S5_GROUPS), f32, minval=math.log(1e-3), maxval=math.log(1e-1)),
        's5_B_re': nrm(ks[13], (NA, S5_GROUPS, S5_STATE, S5_GROUP_CH), (2 * S5_GROUP_CH) ** -0.5),
        's5_B_im': nrm(ks[14], (NA, S5_GROUPS, S5_STATE, S5_GROUP_CH), (2 * S5_GROUP_CH) ** -0.5),
        's5_C_re': nrm(ks[15], (NA, S5_GROUPS, S5_GROUP_CH, S5_STATE), (2 * S5_STATE) ** -0.5),
        's5_C_im': nrm(ks[16], (NA, S5_GROUPS, S5_GROUP_CH, S5_STATE), (2 * S5_STATE) ** -0.5),
        's5_D': nrm(ks[17], (NA, D_MODEL), 0.5),
        's5_w_glu': nrm(ks[18], (NA, D_MODEL, 2 * D_MODEL), D_MODEL ** -0.5),
        'mlstm_w_up': nrm(ks[19], (NB, D_MODEL, 2 * MLSTM_INNER), D_MODEL ** -0.5),
        'mlstm_conv_w': nrm(ks[20], (NB, MLSTM_CONV, MLSTM_INNER), MLSTM_CONV ** -0.5),
        'mlstm_conv_b': nrm(ks[21], (NB, MLSTM_INNER), 0.01),
        'mlstm_wq': nrm(ks[22], (NB, N_QKV_BLOCKS, QKV_BLOCK, QKV_BLOCK), QKV_BLOCK ** -0.5),
        'mlstm_wk': nrm(ks[23], (NB, N_QKV_BLOCKS, QKV_BLOCK, QKV_BLOCK), QKV_BLOCK ** -0.5),
        'mlstm_wv': nrm(ks[24], (NB, N_QKV_BLOCKS, QKV_BLOCK, QKV_BLOCK), QKV_BLOCK ** -0.5),
        'mlstm_w_gate': nrm(ks[25], (NB, 3 * MLSTM_INNER, 2 * MLSTM_HEADS), (3 * MLSTM_INNER) ** -0.5),
        'mlstm_b_gate': b_gate,
        'mlstm_norm_g': 1.0 + nrm(ks[26], (NB, MLSTM_INNER), 0.05),
        'mlstm_skip': 1.0 + nrm(ks[27], (NB, MLSTM_INNER), 0.05),
        'mlstm_w_down': nrm(ks[28], (NB, MLSTM_INNER, D_MODEL), MLSTM_INNER ** -0.5),
        'ffn_w_up': nrm(ks[32], (DEPTH, D_MODEL, 2 * D_FF), D_MODEL ** -0.5),
        'ffn_conv_w': nrm(ks[33], (DEPTH, FFN_CONV, 2 * D_FF), FFN_CONV ** -0.5),
        'ffn_conv_b': nrm(ks[34], (DEPTH, 2 * D_FF), 0.01),
        'ffn_w_down': nrm(ks[35], (DEPTH, D_FF, D_MODEL), D_FF ** -0.5),
    }

def reference(x_prompt, x_sample, state_s5_re, state_s5_im, state_mlstm_C, state_mlstm_n, state_mlstm_m,
              state_mlstm_conv, state_ffn_conv, norm_g, s5_A_re, s5_A_im, s5_log_dt, s5_B_re, s5_B_im,
              s5_C_re, s5_C_im, s5_D, s5_w_glu, mlstm_w_up, mlstm_conv_w, mlstm_conv_b, mlstm_wq, mlstm_wk,
              mlstm_wv, mlstm_w_gate, mlstm_b_gate, mlstm_norm_g, mlstm_skip, mlstm_w_down, ffn_w_up,
              ffn_conv_w, ffn_conv_b, ffn_w_down):
    w = {
        'norm_g': norm_g, 's5_A_re': s5_A_re, 's5_A_im': s5_A_im, 's5_log_dt': s5_log_dt,
        's5_B_re': s5_B_re, 's5_B_im': s5_B_im, 's5_C_re': s5_C_re, 's5_C_im': s5_C_im, 's5_D': s5_D,
        's5_w_glu': s5_w_glu, 'mlstm_w_up': mlstm_w_up, 'mlstm_conv_w': mlstm_conv_w,
        'mlstm_conv_b': mlstm_conv_b, 'mlstm_wq': mlstm_wq, 'mlstm_wk': mlstm_wk, 'mlstm_wv': mlstm_wv,
        'mlstm_w_gate': mlstm_w_gate, 'mlstm_b_gate': mlstm_b_gate, 'mlstm_norm_g': mlstm_norm_g,
        'mlstm_skip': mlstm_skip, 'mlstm_w_down': mlstm_w_down, 'ffn_w_up': ffn_w_up,
        'ffn_conv_w': ffn_conv_w, 'ffn_conv_b': ffn_conv_b, 'ffn_w_down': ffn_w_down,
    }
    f32 = jnp.float32
    pb = x_prompt.shape[0]
    z_s5 = jnp.zeros((N_S5_LAYERS, pb, S5_GROUPS, S5_STATE), f32)
    z_C = jnp.zeros((N_MLSTM_LAYERS, pb, MLSTM_HEADS, MLSTM_HEAD_DIM, MLSTM_HEAD_DIM), f32)
    z_n = jnp.zeros((N_MLSTM_LAYERS, pb, MLSTM_HEADS, MLSTM_HEAD_DIM), f32)
    z_m = jnp.zeros((N_MLSTM_LAYERS, pb, MLSTM_HEADS), f32)
    z_mconv = jnp.zeros((N_MLSTM_LAYERS, pb, MLSTM_CONV - 1, MLSTM_INNER), x_prompt.dtype)
    z_fconv = jnp.zeros((DEPTH, pb, FFN_CONV - 1, 2 * D_FF), x_prompt.dtype)
    y_prompt, p_re, p_im, p_C, p_n, p_m, p_mconv, p_fconv = run_trunk(
        x_prompt, z_s5, z_s5, z_C, z_n, z_m, z_mconv, z_fconv, w)
    y_sample, s_re, s_im, s_C, s_n, s_m, s_mconv, s_fconv = run_trunk(
        x_sample, state_s5_re, state_s5_im, state_mlstm_C, state_mlstm_n, state_mlstm_m,
        state_mlstm_conv, state_ffn_conv, w)
    return (y_prompt, y_sample, p_re, p_im, p_C, p_n, p_m, p_mconv, p_fconv,
            s_re, s_im, s_C, s_n, s_m, s_mconv, s_fconv)


_drawn_inputs = setup_inputs


def setup_inputs(seed=0):
    import zlib

    import numpy as np

    out = dict(_drawn_inputs(seed))
    spreads = {}
    factors = {'s5_A_re': 4.225, 'mlstm_conv_b': 2.822, 'mlstm_skip': 4.016, 'ffn_conv_b': 3.906}
    for name, (base, spread) in spreads.items():
        noise = np.random.default_rng([zlib.crc32(name.encode()), seed]).standard_normal(out[name].shape)
        drawn = base * np.exp(spread * noise) if base else spread * noise
        out[name] = __import__('jax').numpy.asarray(drawn.astype(out[name].dtype))
    for name, factor in factors.items():
        out[name] = (out[name] * factor).astype(out[name].dtype)
    return out
```

```python
from contextlib import ExitStack

import numpy as np
import concourse.bass as bass
from concourse import mybir

F32 = mybir.dt.float32
F32R = mybir.dt.float32r
I32 = mybir.dt.int32
ALU = mybir.AluOpType
ACT = mybir.ActivationFunctionType
AX = mybir.AxisListType

P = 128
D = 1024
KD = D // P
SEQ, STREAMS, STEPS = 1024, 8, 16
T = SEQ + STREAMS * STEPS
NB = 3
TB = T // NB
NORM_EPS, LN_EPS = 1e-6, 1e-5

GROUPS, STATE, CH = 64, 64, 16
L = 8
PC = SEQ // L
SC = STREAMS * STEPS // L
SH = STEPS // L
PAIRS = GROUPS // 2
BATCH = 8

FF = 2816
FT = FF // P
FBLOCKS = FT // 2
FTAPS = 3

INNER, HEADS, DH = 2048, 4, 512
IT = INNER // P
HT = DH // P
MTAPS = 4
QB = 4
CHUNKS = T // P
PCH = SEQ // P


def bcast(ap, axis, n):
    a = ap.unsqueeze(axis)
    return a.broadcast_to([*a.shape[:axis], n, *a.shape[axis + 1:]])


class Env:

    def __init__(self, nc, outer):
        self.nc, self.outer, self.scope = nc, outer, outer
        self.count, self.held = 0, []

    def sb(self, name, shape, dt=F32):
        self.count += 1
        return self.scope.enter_context(self.nc.sbuf_tensor(f"{name}_{self.count}", list(shape), dt))

    def sem(self, name):
        self.count += 1
        handle = self.nc.alloc_semaphore(name=f"{name}_{self.count}")
        self.held.append(handle)
        return handle

    def new_phase(self):
        self.nc.all_engine_barrier()
        self.nc.clear_and_free_semaphores(self.held)
        self.nc.all_engine_barrier()
        self.held = []

    def dram(self, name, shape):
        return self.nc.dram_tensor(name, tuple(shape), F32, kind="Internal").ap()


class Link:

    def __init__(self, eng, sem):
        self.eng, self.sem, self.n = eng, sem, 0

    def __call__(self, ins):
        self.n += 1
        ins.then_inc(self.sem, 1)
        self.eng.wait_ge(self.sem, self.n)


def constants(env):
    nc = env.nc
    env.ident = env.sb("ident", [P, P])
    env.ones = env.sb("ones", [P, P])
    env.cst = env.sb("cst", [P, 4])
    zeroed, made = env.sem("zeroed"), env.sem("made")
    with nc.Block() as block:
        @block.gpsimd
        def _(pool):
            pool.memset(env.ident[:, :], 0.0).then_inc(zeroed, 1)
            pool.memset(env.ones[:, :], 1.0).then_inc(made, 1)
            pool.memset(env.cst[:, 0:1], NORM_EPS).then_inc(made, 1)
            pool.memset(env.cst[:, 1:2], LN_EPS).then_inc(made, 1)
            pool.memset(env.cst[:, 2:3], float(np.pi / 2)).then_inc(made, 1)
            pool.memset(env.cst[:, 3:4], 0.0).then_inc(made, 1)
            pool.wait_ge(zeroed, 1)
            pool.affine_select(out=env.ident[:, :], in_=env.ident[:, :], compare_op=ALU.not_equal, fill=1.0,
                               base=0, pattern=[[-1, P]], channel_multiplier=1).then_inc(made, 1)
    env.eps, env.ln_eps, env.half_pi = env.cst[:, 0:1], env.cst[:, 1:2], env.cst[:, 2:3]


def s5_input(env, x_prompt, x_sample, norm_g, s5_D, u, us, uT):
    nc, bank = env.nc, env.bank
    with ExitStack() as scope:
        env.scope = scope
        gain, skip = env.sb("gain", [P, D]), env.sb("skip", [P, D])
        junk = env.sb("junk", [P, D])
        x, xs = env.sb("x", [P, L, D]), env.sb("xs", [SC, L, D])
        ss, rms, rstd = env.sb("ss", [P, 2 * L]), env.sb("rms", [P, 2 * L]), env.sb("rstd", [P, 2 * L])
        rows = [env.sem(f"rows{j}") for j in range(2)]
        gains, squared, rooted, inverted = env.sem("gains"), env.sem("squared"), env.sem("rooted"), env.sem("inv")
        normed, turned, by_act, by_dve = env.sem("normed"), env.sem("turned"), env.sem("by_act"), env.sem("by_dve")
        own, zero = env.sem("own"), env.sem("zero")
        NBAT = GROUPS // 4
        with nc.Block() as block:
            @block.sync
            def _(sp):
                sp.dma_start(x[:, :, :], x_prompt[0].rearrange("(c j) d -> c j d", j=L)).then_inc(rows[0], 16)
                for h in range(SH):
                    sp.dma_start(xs[STREAMS * h:STREAMS * h + STREAMS, :, :],
                                 x_sample.rearrange("s (h j) d -> h s j d", j=L)[h]).then_inc(rows[1], 16)
                sp.dma_start(gain[:, :], norm_g[0, 0].partition_broadcast(P)).then_inc(gains, 16)
                sp.dma_start(skip[:, :], s5_D[0].partition_broadcast(P)).then_inc(gains, 16)

            @block.scalar
            def _(act):
                act.wait_ge(zero, 1)
                for k in range(2):
                    src, n = (x, P) if k == 0 else (xs, SC)
                    act.wait_ge(rows[k], 16 if k == 0 else 16 * SH)
                    for j in range(L):
                        if k + j:
                            act.wait_ge(own, L * k + j)
                        act.activation(junk[0:n, :], src[:, j, :], ACT.Square,
                                       accum_out=ss[0:n, L * k + j:L * k + j + 1]).then_inc(own, 1)
                act.wait_ge(own, 2 * L)
                act.activation(rms[:, :], ss[:, :], ACT.Sqrt, bias=env.eps, scale=1.0 / D).then_inc(rooted, 1)
                for b in range(0, NBAT, 2):
                    act.wait_ge(turned, b + 1)
                    act.activation(uT[:, 4 * b:4 * b + 4, 0:PC],
                                   bank[b % 4][:, :].rearrange("p (g c) -> p g c", g=4), ACT.Copy).then_inc(by_act, 1)
                act.wait_ge(turned, NBAT + 1)
                act.activation(uT[:, 0:32, PC:PC + SC], bank[4][:, :].rearrange("p (g c) -> p g c", c=SC),
                               ACT.Copy).then_inc(by_act, 1)

            @block.vector
            def _(dve):
                dve.memset(ss[:, :], 0.0).then_inc(zero, 1)
                dve.wait_ge(rooted, 1)
                dve.reciprocal(rstd[:, :], rms[:, :]).then_inc(inverted, 1)
                dve.wait_ge(inverted, 1)
                dve.wait_ge(gains, 32)
                for k in range(2):
                    src, dst, n = (x, u, P) if k == 0 else (xs, us, SC)
                    for j in range(L):
                        q = L * k + j
                        dve.scalar_tensor_tensor(out=dst[:, :, j, :], in0=src[:, j, :].rearrange("p (g c) -> p g c", c=CH),
                                                 scalar=rstd[0:n, q:q + 1],
                                                 in1=gain[0:n, :].rearrange("p (g c) -> p g c", c=CH),
                                                 op0=ALU.mult, op1=ALU.mult).then_inc(normed, 1)
                for b in range(1, NBAT, 2):
                    dve.wait_ge(turned, b + 1)
                    dve.tensor_copy(uT[:, 4 * b:4 * b + 4, 0:PC],
                                    bank[b % 4][:, :].rearrange("p (g c) -> p g c", g=4)).then_inc(by_dve, 1)
                dve.wait_ge(turned, NBAT + 2)
                dve.tensor_copy(uT[:, 32:64, PC:PC + SC],
                                bank[5][:, :].rearrange("p (g c) -> p g c", c=SC)).then_inc(by_dve, 1)
                for src, n in ((u, P), (us, SC)):
                    dve.tensor_tensor(src[:, :, :, :], src[:, :, :, :],
                                      bcast(skip[0:n, :].rearrange("p (g c) -> p g c", c=CH), 2, L), ALU.mult)

            @block.tensor
            def _(pe):
                pe.wait_ge(normed, L)
                for b in range(NBAT):
                    if b >= 4:
                        pe.wait_ge(by_act if b % 2 == 0 else by_dve, (b - 4) // 2 + 1)
                    for k in range(4):
                        g = 4 * b + k
                        m = pe.transpose(bank[b % 4][:, P * k:P * k + P], u[:, g, :, :].rearrange("p j c -> p (j c)"), env.ident[:, :])
                    m.then_inc(turned, 1)
                pe.wait_ge(normed, 2 * L)
                for h in range(2):
                    for k in range(32):
                        g = 32 * h + k
                        m = pe.transpose(bank[4 + h][:, SC * k:SC * k + SC], us[:, g, :, :].rearrange("p j c -> p (j c)"),
                                         env.ident[0:SC, 0:SC])
                    m.then_inc(turned, 1)


def s5_matrices(env, a_re, a_im, log_dt, c_re, c_im, b_re, b_im, h_re, h_im, pw, bb, wo, ss, sss):
    nc, bank = env.nc, env.bank
    with ExitStack() as scope:
        env.scope = scope
        raw = env.sb("raw", [PAIRS, 3, P])
        dtr, dte = env.sb("dtr", [PAIRS, 2]), env.sb("dte", [PAIRS, 2])
        crow = env.sb("crow", [P, 2, 8, STATE])
        brow = env.sb("brow", [P, 2, PAIRS, CH])
        hrow = env.sb("hrow", [P, 2, 2, P])
        ct = env.sb("ct", [P, 2, PAIRS, CH])
        a = env.sb("a", [P, 3, PAIRS])
        w = env.sb("w", [P, 16, PAIRS])
        wi = env.sb("wi", [P, PAIRS], I32)
        big = env.sb("big", [P, PAIRS, CH])
        loaded = [env.sem(f"loaded{k}") for k in range(4)]
        dt_ready, spread, turned = env.sem("dt_ready"), env.sem("spread"), env.sem("turned")
        own, sines, angle = env.sem("own"), env.sem("sines"), env.sem("angle")
        with nc.Block() as block:
            @block.sync
            def _(sp):
                sp.dma_start(raw[:, 0, :], a_re[0].rearrange("(p g) n -> p (g n)", g=2)).then_inc(loaded[0], 16)
                sp.dma_start(raw[:, 1, :], a_im[0].rearrange("(p g) n -> p (g n)", g=2)).then_inc(loaded[0], 16)
                sp.dma_start(dtr[:, :], log_dt[0].rearrange("(p g) -> p g", g=2)).then_inc(loaded[0], 16)
                for k, c in enumerate((c_re, c_im)):
                    sp.dma_start(crow[:, k, :, :],
                                 c[0].rearrange("g c n -> (g c) n").rearrange("(q r) n -> r q n", r=P)).then_inc(loaded[1], 16)
                for k, h in enumerate((h_re, h_im)):
                    sp.dma_start(hrow[:, k, :, :], h[0].rearrange("s g n -> (s g n)").rearrange(
                        "(b q m) -> q b m", b=2, m=P)).then_inc(loaded[2], 16)

            @block.gpsimd
            def _(pool):
                for k, b in enumerate((b_re, b_im)):
                    pool.dma_start(brow[:, k, :, :], b[0].rearrange("(p g) n c -> (g n) p c", g=2)).then_inc(loaded[3], 16)

            @block.tensor
            def _(pe):
                pe.wait_ge(spread, 1)
                pe.wait_ge(loaded[0], 48)
                for k in range(3):
                    m = pe.transpose(bank[0][:, PAIRS * k:PAIRS * k + PAIRS], raw[:, k, :], env.ident[0:PAIRS, 0:PAIRS])
                m.then_inc(turned, 1)
                pe.wait_ge(loaded[1], 32)
                for k in range(2):
                    for q in range(8):
                        for g in range(2):
                            m = pe.matmul(bank[1 + 2 * k + q // 4][STATE * g:STATE * g + STATE, P * (q % 4):P * (q % 4) + P],
                                          crow[:, k, q, :], env.ident[:, :], start=True, stop=True)
                m.then_inc(turned, 1)
                pe.wait_ge(loaded[2], 32)
                for k in range(2):
                    for q in range(2):
                        m = pe.transpose(bank[5][:, P * (2 * k + q):P * (2 * k + q) + P], hrow[:, k, q, :], env.ident[:, :])
                m.then_inc(turned, 1)

            @block.scalar
            def _(act):
                act.wait_ge(loaded[0], 48)
                act.activation(dte[:, :], dtr[:, :], ACT.Exp).then_inc(dt_ready, 1)
                act.wait_ge(angle, 1)
                act.activation(w[:, 3, :], w[:, 2, :], ACT.Sin, scale=0.5).then_inc(sines, 1)
                act.activation(w[:, 4, :], w[:, 2, :], ACT.Abs, scale=0.5).then_inc(own, 1)
                act.wait_ge(own, 1)
                act.activation(w[:, 5, :], w[:, 4, :], ACT.Sin, bias=env.half_pi, scale=-1.0).then_inc(sines, 1)
                act.activation(w[:, 0, :], w[:, 1, :], ACT.Exp).then_inc(sines, 1)

            @block.vector
            def _(dve):
                link = Link(dve, env.sem("link"))
                dve.wait_ge(dt_ready, 1)
                dve.tensor_copy(raw[:, 2, :].rearrange("p (g n) -> p g n", g=2), bcast(dte[:, :], 2, STATE)).then_inc(spread, 1)
                dve.wait_ge(turned, 1)
                link(dve.tensor_copy(a[:, :, :], bank[0][:, 0:3 * PAIRS].rearrange("p (k q) -> p k q", k=3)))
                tt, ts = dve.tensor_tensor, dve.tensor_scalar
                link(tt(w[:, 1, :], a[:, 0, :], a[:, 2, :], ALU.mult))
                link(tt(w[:, 2, :], a[:, 1, :], a[:, 2, :], ALU.mult))
                link(ts(wi[:, :], w[:, 2, :], float(1 / (2 * np.pi)), None, ALU.mult))
                link(dve.tensor_copy(w[:, 6, :], wi[:, :]))
                rest = 2 * np.pi
                for k in range(3):
                    part = float(np.float32(np.round(rest * 2.0 ** (7 + 11 * k)) / 2.0 ** (7 + 11 * k))) if k < 2 else float(np.float32(rest))
                    rest -= part
                    link(ts(w[:, 7, :], w[:, 6, :], -part, None, ALU.mult))
                    ins = tt(w[:, 2, :], w[:, 2, :], w[:, 7, :], ALU.add)
                    if k < 2:
                        link(ins)
                ins.then_inc(angle, 1)
                dve.wait_ge(sines, 3)
                link(tt(w[:, 6, :], w[:, 3, :], w[:, 5, :], ALU.mult))
                link(tt(w[:, 7, :], w[:, 3, :], w[:, 3, :], ALU.mult))
                link(ts(w[:, 7, :], w[:, 7, :], -2.0, 1.0, ALU.mult, ALU.add))
                link(tt(pw[:, 0, 1, :], w[:, 0, :], w[:, 7, :], ALU.mult))
                link(dve.scalar_tensor_tensor(out=pw[:, 1, 1, :], in0=w[:, 6, :], scalar=2.0, in1=w[:, 0, :],
                                              op0=ALU.mult, op1=ALU.mult))
                link(dve.memset(pw[:, 0, 0, :], 1.0))
                link(dve.memset(pw[:, 1, 0, :], 0.0))
                for k in range(2, L + 1):
                    link(tt(pw[:, 0, k, :], pw[:, 0, k - 1, :], pw[:, 0, 1, :], ALU.mult))
                    link(tt(w[:, 6, :], pw[:, 1, k - 1, :], pw[:, 1, 1, :], ALU.mult))
                    link(tt(pw[:, 0, k, :], pw[:, 0, k, :], w[:, 6, :], ALU.subtract))
                    link(tt(pw[:, 1, k, :], pw[:, 0, k - 1, :], pw[:, 1, 1, :], ALU.mult))
                    link(tt(w[:, 6, :], pw[:, 1, k - 1, :], pw[:, 0, 1, :], ALU.mult))
                    link(tt(pw[:, 1, k, :], pw[:, 1, k, :], w[:, 6, :], ALU.add))
                link(ts(w[:, 8, :], pw[:, 0, 1, :], -1.0, None, ALU.add))
                link(tt(w[:, 9, :], a[:, 0, :], a[:, 0, :], ALU.mult))
                link(tt(w[:, 10, :], a[:, 1, :], a[:, 1, :], ALU.mult))
                link(tt(w[:, 9, :], w[:, 9, :], w[:, 10, :], ALU.add))
                link(dve.reciprocal(w[:, 9, :], w[:, 9, :]))
                link(tt(w[:, 10, :], w[:, 8, :], a[:, 0, :], ALU.mult))
                link(tt(w[:, 11, :], pw[:, 1, 1, :], a[:, 1, :], ALU.mult))
                link(tt(w[:, 10, :], w[:, 10, :], w[:, 11, :], ALU.add))
                link(tt(w[:, 10, :], w[:, 10, :], w[:, 9, :], ALU.mult))
                link(tt(w[:, 11, :], pw[:, 1, 1, :], a[:, 0, :], ALU.mult))
                link(tt(w[:, 12, :], w[:, 8, :], a[:, 1, :], ALU.mult))
                link(tt(w[:, 11, :], w[:, 11, :], w[:, 12, :], ALU.subtract))
                link(tt(w[:, 11, :], w[:, 11, :], w[:, 9, :], ALU.mult))
                dve.wait_ge(loaded[3], 32)
                br, bi = brow[:, 0, :, :], brow[:, 1, :, :]
                fr, fi = bcast(w[:, 10, :], 2, CH), bcast(w[:, 11, :], 2, CH)
                for o, (x0, x1, op) in enumerate(((br, bi, ALU.subtract), (bi, br, ALU.add))):
                    link(tt(bb[:, o, :, :], x0, fr, ALU.mult))
                    link(tt(big[:, :, :], x1, fi, ALU.mult))
                    link(tt(bb[:, o, :, :], bb[:, o, :, :], big[:, :, :], op))
                dve.wait_ge(turned, 2)
                for k in range(2):
                    for h in range(2):
                        for g in range(2):
                            src = bank[1 + 2 * k + h][STATE * g:STATE * g + STATE, :].rearrange("n (p g c) -> n p g c", g=2, c=CH)
                            link(dve.tensor_copy(ct[STATE * g:STATE * g + STATE, k, 16 * h:16 * h + 16, :], src[:, :, g, :]))
                for k in range(L + 1):
                    pr, pi = bcast(pw[:, 0, k, :], 2, CH), bcast(pw[:, 1, k, :], 2, CH)
                    link(tt(wo[:, 0, :, k, :], ct[:, 0, :, :], pr, ALU.mult))
                    link(tt(big[:, :, :], ct[:, 1, :, :], pi, ALU.mult))
                    link(tt(wo[:, 0, :, k, :], wo[:, 0, :, k, :], big[:, :, :], ALU.subtract))
                    link(tt(wo[:, 1, :, k, :], ct[:, 1, :, :], pr, ALU.mult))
                    link(tt(big[:, :, :], ct[:, 0, :, :], pi, ALU.mult))
                    link(dve.scalar_tensor_tensor(out=wo[:, 1, :, k, :], in0=wo[:, 1, :, k, :], scalar=-1.0,
                                                  in1=big[:, :, :], op0=ALU.mult, op1=ALU.subtract))
                link(dve.memset(ss[:, :, :, 0:1], 0.0))
                dve.wait_ge(turned, 3)
                for k in range(2):
                    link(dve.tensor_copy(sss[:, k, :, 0, :].rearrange("p q s -> p s q"),
                                         bank[5][:, 2 * P * k:2 * P * k + 2 * P].rearrange("p (s q) -> p s q", q=PAIRS)))


def s5_states(env, uT, pw, bb, ss, sss):
    nc, bank = env.nc, env.bank
    NBAT = PAIRS // BATCH
    CW = PC + SC
    with ExitStack() as scope:
        env.scope = scope
        bar = env.sb("bar", [P, 2, BATCH, L, CH])
        tmp = env.sb("tmp", [P, BATCH, L, CH])
        wt = env.sb("wt", [P, 2, BATCH, P])
        step = env.sb("step", [P, 2, PAIRS])
        t4 = env.sb("t4", [P, 2, 2, PAIRS])
        t4s = env.sb("t4s", [P, 2, 2, PAIRS, STREAMS])
        made, turned, copied, multiplied = env.sem("made"), env.sem("turned"), env.sem("copied"), env.sem("multiplied")
        left, steps = env.sem("left"), env.sem("steps")
        with nc.Block() as block:
            @block.vector
            def _(dve):
                link = Link(dve, env.sem("link"))
                tt = dve.tensor_tensor
                link(dve.tensor_copy(step[:, :, :], pw[:, :, L, :]))
                dve.memset(t4[:, :, :, :], 0.0).then_inc(steps, 1)
                for b in range(NBAT):
                    ps = slice(BATCH * b, BATCH * b + BATCH)
                    if b:
                        dve.wait_ge(turned, b)
                    for o, op in ((0, ALU.subtract), (1, ALU.add)):
                        for j in range(L):
                            pr, pi = bcast(pw[:, 0, L - 1 - j, ps], 2, CH), bcast(pw[:, 1, L - 1 - j, ps], 2, CH)
                            link(tt(bar[:, o, :, j, :], bb[:, o, ps, :], pr, ALU.mult))
                            link(tt(tmp[:, :, j, :], bb[:, 1 - o, ps, :], pi, ALU.mult))
                        ins = tt(bar[:, o, :, :, :].rearrange("p a b c -> p (a b c)"),
                                 bar[:, o, :, :, :].rearrange("p a b c -> p (a b c)"),
                                 tmp[:, :, :, :].rearrange("p a b c -> p (a b c)"), op)
                        if o == 0:
                            link(ins)
                    ins.then_inc(made, 1)
                dve.wait_ge(left, PAIRS)
                n0 = 0
                with dve.Fori(0, PC) as c:
                    now = ss[:, :, :, bass.ds(c, 1)].rearrange("p r q o -> p r (q o)")
                    then = ss[:, :, :, bass.ds(c + 1, 1)].rearrange("p r q o -> p r (q o)")
                    dve.wait_ge(steps, c * 4 + 1)
                    tt(t4[:, 0, :, :], bcast(step[:, 0, :], 1, 2), now, ALU.mult).then_inc(steps, 1)
                    tt(t4[:, 1, :, :], bcast(step[:, 1, :], 1, 2), now, ALU.mult).then_inc(steps, 1)
                    dve.wait_ge(steps, c * 4 + 3)
                    tt(then, then, t4[:, 0, :, :], ALU.add).then_inc(steps, 1)
                    dve.wait_ge(steps, c * 4 + 4)
                    ti = t4[:, 1, :, :]
                    tt(then[:, 0, :], then[:, 0, :], ti[:, 1, :], ALU.subtract)
                    tt(then[:, 1, :], then[:, 1, :], ti[:, 0, :], ALU.add).then_inc(steps, 1)
                for c in range(SH):
                    for k in range(2):
                        for r in range(2):
                            link(tt(t4s[:, k, r, :, :], bcast(step[:, k, :], 2, STREAMS), sss[:, r, :, c, :], ALU.mult))
                    for r in range(2):
                        link(tt(sss[:, r, :, c + 1, :], sss[:, r, :, c + 1, :], t4s[:, 0, r, :, :], ALU.add))
                        link(tt(sss[:, r, :, c + 1, :], sss[:, r, :, c + 1, :], t4s[:, 1, 1 - r, :, :],
                                ALU.subtract if r == 0 else ALU.add))

            @block.scalar
            def _(act):
                for b in range(NBAT):
                    act.wait_ge(turned, b + 1)
                    if b:
                        act.wait_ge(multiplied, BATCH * b)
                    for k in range(4):
                        act.activation(wt[:, k // 2, 4 * (k % 2):4 * (k % 2) + 4, :],
                                       bank[k][:, :].rearrange("p (q m) -> p q m", q=4), ACT.Copy).then_inc(copied, 1)
                    for p in range(BATCH * b, BATCH * b + BATCH):
                        act.wait_ge(multiplied, p + 1)
                        sums = bank[4 + p % 4][:, 0:2 * CW].rearrange("n (r c) -> n r c", r=2)
                        act.activation(sss[:, :, p, 1:, :].rearrange("n r h s -> n r (h s)"), sums[:, :, PC:], ACT.Copy)
                        act.activation(ss[:, :, p, 1:], sums[:, :, 0:PC], ACT.Copy).then_inc(left, 1)

            @block.tensor
            def _(pe):
                for b in range(NBAT):
                    pe.wait_ge(made, b + 1)
                    if b:
                        pe.wait_ge(copied, 4 * b)
                    for o in range(2):
                        for q in range(BATCH):
                            m = pe.transpose(bank[2 * o + q // 4][:, P * (q % 4):P * (q % 4) + P],
                                             bar[:, o, q, :, :].rearrange("p j c -> p (j c)"), env.ident[:, :])
                    m.then_inc(turned, 1)
                    pe.wait_ge(copied, 4 * b + 4)
                    for q in range(BATCH):
                        p = BATCH * b + q
                        if p >= 4:
                            pe.wait_ge(left, p - 3)
                        for o in range(2):
                            for g in range(2):
                                m = pe.matmul(bank[4 + p % 4][STATE * g:STATE * g + STATE, CW * o:CW * o + CW],
                                              wt[:, o, q, STATE * g:STATE * g + STATE], uT[:, 2 * p + g, :],
                                              start=True, stop=True)
                        m.then_inc(multiplied, 1)


def s5_output(env, uT, u, us, bb, wo, ss, sss, outs):
    nc, bank = env.nc, env.bank
    BATCH = 4
    NBAT = PAIRS // BATCH
    G = 2 * BATCH
    Q = 2
    with ExitStack() as scope:
        env.scope = scope
        kk = env.sb("kk", [CH, G, P])
        toep = [env.sb(f"toep{k}", [P, G, P]) for k in range(2)]
        fin_p = env.sb("fin_p", [PAIRS, 2, P])
        fin_s = env.sb("fin_s", [P, 2, 2, P])
        last = env.sb("last", [P, 2, STREAMS, PAIRS])
        packed = env.sem("packed")
        cleared, lagged, kept = env.sem("cleared"), env.sem("lagged"), env.sem("kept")
        placed = [env.sem(f"placed{k}") for k in range(2)]
        summed, added, added_s, stored = (env.sem(n) for n in ("summed", "added", "added_s", "stored"))
        turned, ended = env.sem("turned"), env.sem("ended")
        with nc.Block() as block:
            @block.gpsimd
            def _(pool):
                for k in range(2):
                    pool.memset(toep[k][:, :, :], 0.0).then_inc(cleared, 1)

            @block.sync
            def _(sp):
                sp.wait_ge(cleared, 2)
                for b in range(NBAT):
                    sp.wait_ge(kept, Q * (b + 1))
                    if b >= 2:
                        sp.wait_ge(summed, Q * (b - 1))
                    for j in range(L):
                        sp.dma_start(toep[b % 2][CH * j:CH * j + CH, :, CH * j:P],
                                     kk[:, :, 0:P - CH * j]).then_inc(placed[b % 2], 16)
                sp.wait_ge(ended, 2)
                for k in range(2):
                    sp.dma_start(outs[k][0, 0].rearrange("g n -> (g n)").rearrange("(p m) -> p m", m=P),
                                 fin_p[:, k, :]).then_inc(stored, 16)
                    sp.dma_start(outs[2 + k][0].rearrange("s g n -> (s g n)").rearrange("(b q m) -> q b m", b=2, m=P),
                                 fin_s[:, k, :, :]).then_inc(stored, 16)
                sp.wait_ge(stored, 16 * 4)

            @block.tensor
            def _(pe):
                def lags(b):
                    if b:
                        pe.wait_ge(kept, Q * b)
                    for g in range(Q):
                        rows = slice(STATE * g, STATE * g + STATE)
                        for h in range(BATCH):
                            p = BATCH * b + h
                            for o in range(2):
                                m = pe.matmul(bank[g][0:CH, P * h:P * h + P], bb[rows, o, p, :],
                                              wo[rows, o, p, 0:L, :].rearrange("p k c -> p (k c)"),
                                              start=(o == 0), stop=(o == 1))
                        m.then_inc(lagged, 1)

                def outputs(b):
                    pe.wait_ge(placed[b % 2], 16 * L * (b // 2 + 1))
                    for f in range(Q):
                        n = Q * b + f
                        if n >= 2:
                            pe.wait_ge(added, n - 1)
                            pe.wait_ge(added_s, n - 1)
                        for h in range(BATCH):
                            p, g = BATCH * b + h, f
                            rows = slice(STATE * g, STATE * g + STATE)
                            cols = slice(P * h, P * h + P)
                            t = toep[b % 2][:, 4 * f + h, :]
                            for dst, x, s in ((bank[4 + n % 2][:, cols], uT[:, 2 * p + g, 0:PC], [ss[rows, o, p, 0:PC] for o in range(2)]),
                                              (bank[6 + n % 2][0:SC, cols], uT[:, 2 * p + g, PC:], [sss[rows, o, p, 0:SH, :].rearrange("n h s -> n (h s)") for o in range(2)])):
                                pe.matmul(dst, x, t, start=True, stop=False)
                                for o in range(2):
                                    m = pe.matmul(dst, s[o], wo[rows, o, p, 1:, :].rearrange("p k c -> p (k c)"),
                                                  start=False, stop=(o == 1))
                        m.then_inc(summed, 1)

                lags(0)
                for b in range(NBAT):
                    if b + 1 < NBAT:
                        lags(b + 1)
                    outputs(b)
                pe.wait_ge(kept, Q * NBAT)
                pe.wait_ge(packed, 2)
                for o in range(2):
                    pe.transpose(bank[0][0:PAIRS, P * o:P * o + P], ss[:, o, :, PC], env.ident[:, :])
                    for h in range(2):
                        m = pe.transpose(bank[1][:, P * (2 * o + h):P * (2 * o + h) + P],
                                         last[:, o, 4 * h:4 * h + 4, :].rearrange("p s q -> p (s q)"), env.ident[:, :])
                m.then_inc(turned, 1)

            @block.scalar
            def _(act):
                for b in range(NBAT):
                    for f in range(Q):
                        act.wait_ge(lagged, Q * b + f + 1)
                        if b and f == 0:
                            act.wait_ge(placed[(b - 1) % 2], 16 * L * ((b - 1) // 2 + 1))
                        act.activation(kk[:, 4 * f:4 * f + 4, :], bank[f][0:CH, :].rearrange("p (g m) -> p g m", g=4),
                                       ACT.Copy).then_inc(kept, 1)

            @block.vector
            def _(dve):
                for o in range(2):
                    dve.tensor_copy(last[:, o, :, :].rearrange("p s q -> p q s"), sss[:, o, :, SH, :]).then_inc(packed, 1)
                for n in range(GROUPS // 4):
                    dve.wait_ge(summed, n + 1)
                    for dst, src, sem in ((u, bank[4 + n % 2][:, :], added), (us, bank[6 + n % 2][0:SC, :], added_s)):
                        g0 = G * (n // Q) + n % Q
                        y = dst[:, g0:g0 + G - 1:Q, :, :].rearrange("p g t c -> p g (t c)")
                        dve.tensor_tensor(y, y, src.rearrange("p (g m) -> p g m", m=P), ALU.add).then_inc(sem, 1)
                dve.wait_ge(turned, 1)
                dve.tensor_copy(fin_p[:, :, :], bank[0][0:PAIRS, 0:2 * P].rearrange("p (o m) -> p o m", o=2)).then_inc(ended, 1)
                dve.tensor_copy(fin_s[:, :, :, :].rearrange("p a b m -> p (a b m)"), bank[1][:, :]).then_inc(ended, 1)


def s5_gelu(env, u, us, z_rows):
    nc = env.nc
    with ExitStack() as scope:
        env.scope = scope
        z = [env.sb(f"z{k}", [P, GROUPS, CH]) for k in range(4)]
        gelu = env.sem("gelu")
        stored = [env.sem(f"stored{k}") for k in range(4)]
        with nc.Block() as block:
            @block.scalar
            def _(act):
                for q in range(2 * L):
                    if q >= 4:
                        act.wait_ge(stored[q % 4], 16 * (q // 4) if q % 2 == 0 else 16 * SH * (q // 4))
                    src, n = (u, P) if q % 2 == 0 else (us, SC)
                    act.activation(z[q % 4][0:n, :, :], src[:, :, q // 2, :], ACT.Gelu_apprx_tanh).then_inc(gelu, 1)

            @block.sync
            def _(sp):
                for q in range(2 * L):
                    sp.wait_ge(gelu, q + 1)
                    j, src = q // 2, z[q % 4][:, :, :].rearrange("p g c -> p (g c)")
                    if q % 2 == 0:
                        sp.dma_start(z_rows[0:SEQ, :].rearrange("(c j) d -> c j d", j=L)[:, j, :], src).then_inc(stored[q % 4], 16)
                    else:
                        for h in range(SH):
                            sp.dma_start(z_rows[SEQ:T, :].rearrange("(s h j) d -> h s j d", h=SH, j=L)[h, :, j, :],
                                         src[STREAMS * h:STREAMS * h + STREAMS, :]).then_inc(stored[q % 4], 16)
                for k in range(4):
                    sp.wait_ge(stored[k], 16 * (L // 2) * (1 if k % 2 == 0 else SH))


def s5(env, i, z_rows, outs):
    with ExitStack() as scope:
        env.scope = scope
        u, us = env.sb("u", [P, GROUPS, L, CH]), env.sb("us", [SC, GROUPS, L, CH])
        uT = env.sb("uT", [P, GROUPS, PC + SC])
        s5_input(env, i["x_prompt"], i["x_sample"], i["norm_g"], i["s5_D"], u, us, uT)
        env.scope = scope
        bb = env.sb("bb", [P, 2, PAIRS, CH])
        wo = env.sb("wo", [P, 2, PAIRS, L + 1, CH])
        ss, sss = env.sb("ss", [P, 2, PAIRS, PC + 1]), env.sb("sss", [P, 2, PAIRS, SH + 1, STREAMS])
        with ExitStack() as inner:
            env.scope = inner
            pw = env.sb("pw", [P, 2, L + 1, PAIRS])
            s5_matrices(env, i["s5_A_re"], i["s5_A_im"], i["s5_log_dt"], i["s5_C_re"], i["s5_C_im"],
                        i["s5_B_re"], i["s5_B_im"], i["state_s5_re"], i["state_s5_im"], pw, bb, wo, ss, sss)
            env.scope = inner
            s5_states(env, uT, pw, bb, ss, sss)
        s5_output(env, uT, u, us, bb, wo, ss, sss, outs)
        s5_gelu(env, u, us, z_rows)


def held(eng, counter):
    eng.sem_inc(counter, 1)


class Weights:

    def __init__(self, env):
        self.raw = [env.sb(f"w_raw{k}", [P, D]) for k in range(2)]
        self.head = [env.sb(f"w_head{k}", [P, D], F32R) for k in range(2)]
        self.rest = [env.sb(f"w_rest{k}", [P, D], F32R) for k in range(2)]
        self.landed = [env.sem(f"w_landed{k}") for k in range(2)]
        self.rounded, self.split, self.used = env.sem("w_rounded"), env.sem("w_split"), env.sem("w_used")
        self.freed = env.sem("w_freed")

    def load(self, sp, n, slot, src, first=False):
        if not first:
            sp.wait_ge(self.split, n - 1)
            held(sp, self.freed)
        sp.dma_start(self.raw[slot][:, :].rearrange("p (a b) -> p a b", a=src.shape[1]), src).then_inc(self.landed[slot], 16)

    def _arrived(self, eng, n, slot, first):
        eng.wait_ge(self.landed[slot], 8 * n + 16 - 8 * slot)
        if not first:
            eng.wait_ge(self.used, n - 1)

    def round(self, act, n, slot, first=False):
        self._arrived(act, n, slot, first)
        act.activation(self.head[slot][:, :], self.raw[slot][:, :], ACT.Copy).then_inc(self.rounded, 1)

    def subtract(self, dve, n, slot, first=False):
        dve.wait_ge(self.rounded, n + 1)
        dve.tensor_tensor(self.rest[slot][:, :], self.raw[slot][:, :], self.head[slot][:, :].bitcast(F32),
                          ALU.subtract).then_inc(self.split, 1)

    def ready(self, pe, n):
        pe.wait_ge(self.rounded, n + 1)
        pe.wait_ge(self.split, n + 1)


def up_tile(pe, env, n, slot, x_head, x_rest, banks):
    w = env.w
    w.ready(pe, n)
    for k in range(KD):
        for lhs, rhs, first, last in ((w.head, x_head, k == 0, False), (w.head, x_rest, False, False),
                                      (w.rest, x_head, False, k == KD - 1)):
            for c in range(NB):
                m = pe.matmul(banks[c][:, 0:TB], lhs[slot][:, P * k:P * k + P], rhs[:, k, TB * c:TB * c + TB],
                              start=first, stop=last)
    m.then_inc(w.used, 1)


def rows_in(env, z_rows, x_prompt, x_sample, x_dram, h_head, h_rest):
    nc, bank = env.nc, env.bank
    with ExitStack() as scope:
        env.scope = scope
        zr = [env.sb(f"zr{k}", [P, D]) for k in range(2)]
        xr = [env.sb(f"xr{k}", [P, D]) for k in range(2)]
        xt = env.sb("xt", [P, KD, T])
        z_in = [env.sem(f"z_in{k}") for k in range(2)]
        x_in = [env.sem(f"x_in{k}") for k in range(2)]
        z_turned, x_turned, head, rest, x_out, stored = (env.sem(n) for n in ("z_turned", "x_turned", "head", "rest", "x_out", "stored"))
        R = T // P
        xp, xs = x_prompt[0], x_sample.rearrange("s j d -> (s j) d")
        with nc.Block() as block:
            @block.sync
            def _(sp):
                for r in range(R):
                    k = r % 2
                    if r >= 2:
                        sp.wait_ge(z_turned, 2 * (r - 1))
                        sp.wait_ge(x_turned, 2 * (r - 1))
                    sp.dma_start(zr[k][:, :], z_rows[P * r:P * r + P, :]).then_inc(z_in[k], 16)
                    sp.dma_start(xr[k][:, :], xp[P * r:P * r + P, :] if r < SEQ // P else xs).then_inc(x_in[k], 16)
                sp.wait_ge(x_out, 2 * R)
                sp.dma_start(x_dram.rearrange("k p t -> p k t"), xt[:, :, :]).then_inc(stored, 16)
                sp.wait_ge(stored, 16)

            @block.tensor
            def _(pe):
                for r in range(R):
                    k = r % 2
                    pe.wait_ge(z_in[k], 16 * (r // 2 + 1))
                    for h in range(2):
                        if r >= 2:
                            pe.wait_ge(head, 2 * (r - 2) + h + 1)
                            pe.wait_ge(rest, 2 * (r - 2) + h + 1)
                        for q in range(4):
                            c = P * (4 * h + q)
                            m = pe.transpose(bank[2 * k + h][:, P * q:P * q + P], zr[k][:, c:c + P], env.ident[:, :])
                        m.then_inc(z_turned, 1)
                    pe.wait_ge(x_in[k], 16 * (r // 2 + 1))
                    for h in range(2):
                        if r >= 2:
                            pe.wait_ge(x_out, 2 * (r - 2) + h + 1)
                        for q in range(4):
                            c = P * (4 * h + q)
                            m = pe.transpose(bank[4 + 2 * k + h][:, P * q:P * q + P], xr[k][:, c:c + P], env.ident[:, :])
                        m.then_inc(x_turned, 1)

            @block.scalar
            def _(act):
                for r in range(R):
                    for h in range(2):
                        act.wait_ge(z_turned, 2 * r + h + 1)
                        act.activation(h_head[:, 4 * h:4 * h + 4, P * r:P * r + P],
                                       bank[2 * (r % 2) + h][:, :].rearrange("p (q t) -> p q t", q=4), ACT.Copy).then_inc(head, 1)
                    for h in range(2):
                        act.wait_ge(x_turned, 2 * r + h + 1)
                        act.activation(xt[:, 4 * h:4 * h + 4, P * r:P * r + P],
                                       bank[4 + 2 * (r % 2) + h][:, :].rearrange("p (q t) -> p q t", q=4), ACT.Copy).then_inc(x_out, 1)

            @block.vector
            def _(dve):
                for r in range(R):
                    for h in range(2):
                        dve.wait_ge(head, 2 * r + h + 1)
                        dve.tensor_tensor(h_rest[:, 4 * h:4 * h + 4, P * r:P * r + P],
                                          bank[2 * (r % 2) + h][:, :].rearrange("p (q t) -> p q t", q=4),
                                          h_head[:, 4 * h:4 * h + 4, P * r:P * r + P].bitcast(F32),
                                          ALU.subtract).then_inc(rest, 1)


def gains_in(env, norm_g):
    nc, bank = env.nc, env.bank
    with ExitStack() as scope:
        env.scope = scope
        rows = env.sb("rows", [8, D])
        landed, turned, done = env.sem("landed"), env.sem("turned"), env.sem("done")
        with nc.Block() as block:
            @block.sync
            def _(sp):
                sp.dma_start(rows[:, :], norm_g.rearrange("l w d -> (l w) d")).then_inc(landed, 16)

            @block.tensor
            def _(pe):
                pe.wait_ge(landed, 16)
                for k in range(KD):
                    m = pe.transpose(bank[0][:, 8 * k:8 * k + 8], rows[:, P * k:P * k + P], env.ident[0:8, 0:8])
                m.then_inc(turned, 1)

            @block.vector
            def _(dve):
                dve.wait_ge(turned, 1)
                dve.tensor_copy(env.gains[:, :, :].rearrange("p k w -> p (k w)"), bank[0][:, 0:8 * KD]).then_inc(done, 1)


def glu(env, w_glu, x_head, x_rest, f):
    nc, w, banks = env.nc, env.w, [env.bank[0:NB], env.bank[NB:2 * NB]]
    n0 = env.units
    src = w_glu[0].rearrange("(k p) m -> p k m", p=P)
    with ExitStack() as scope:
        env.scope = scope
        gate = env.sb("gate", [P, T])
        gated, free = env.sem("gated"), env.sem("free")
        with nc.Block() as block:
            @block.sync
            def _(sp):
                for h in range(2):
                    w.load(sp, n0 + h, h, src[:, :, D * (1 - h):D * (1 - h) + P], first=(n0 == 0))
                with sp.Fori(1, KD) as m:
                    for h in range(2):
                        w.load(sp, m * 2 + (n0 + h), h, src[:, :, bass.ds(m * P + D * (1 - h), P)])

            @block.tensor
            def _(pe):
                for h in range(2):
                    up_tile(pe, env, n0 + h, h, x_head, x_rest, banks[h])
                with pe.Fori(1, KD) as m:
                    pe.wait_ge(gated, m * NB)
                    up_tile(pe, env, m * 2 + n0, 0, x_head, x_rest, banks[0])
                    pe.wait_ge(free, m * NB)
                    up_tile(pe, env, m * 2 + (n0 + 1), 1, x_head, x_rest, banks[1])

            @block.scalar
            def _(act):
                w.round(act, n0, 0, first=(n0 == 0))
                w.round(act, n0 + 1, 1, first=(n0 == 0))

                def gates(m):
                    act.wait_ge(w.used, m * 2 + (n0 + 1))
                    if not isinstance(m, int) or m:
                        act.wait_ge(free, m * NB)
                    for c in range(NB):
                        act.activation(gate[:, TB * c:TB * c + TB], banks[0][c][:, 0:TB], ACT.Sigmoid).then_inc(gated, 1)

                gates(0)
                for h in range(2):
                    w.round(act, n0 + 2 + h, h)
                with act.Fori(1, KD - 1) as m:
                    gates(m)
                    for h in range(2):
                        w.round(act, m * 2 + (n0 + 2 + h), h)
                gates(KD - 1)

            @block.vector
            def _(dve):
                def values(m, n):
                    dve.wait_ge(w.used, n)
                    for c in range(NB):
                        dve.wait_ge(gated, m * NB + (c + 1))
                        dve.tensor_tensor(f[:, m, TB * c:TB * c + TB] if isinstance(m, int) else
                                          f[:, bass.ds(m, 1), TB * c:TB * c + TB].rearrange("p o t -> p (o t)"),
                                          banks[1][c][:, 0:TB], gate[:, TB * c:TB * c + TB], ALU.mult).then_inc(free, 1)

                w.subtract(dve, n0, 0)
                w.subtract(dve, n0 + 1, 1)
                with dve.Fori(0, KD - 1) as m:
                    for h in range(2):
                        w.subtract(dve, m * 2 + (n0 + 2 + h), h)
                    values(m, m * 2 + (n0 + 2))
                values(KD - 1, n0 + 2 * KD)
    env.units = n0 + 2 * KD


def norm_add_norm(env, f, x_dram, post, pre, h_head=None, h_rest=None, y=None):
    nc, bank = env.nc, env.bank
    final = pre is None
    with ExitStack() as scope:
        env.scope = scope
        x = [env.sb(f"x{k}", [P, KD, TB]) for k in range(2)]
        sq = [env.sb(f"sq{k}", [P, TB]) for k in range(4)]
        tmp = [env.sb(f"tmp{k}", [P, TB]) for k in range(4)]
        root = env.sb("root", [P, TB])
        inv = [env.sb(f"inv{k}", [P, TB]) for k in range(2)]
        x_in = [env.sem(f"x_in{k}") for k in range(2)]
        squared, summed, rooted, inverted = env.sem("squared"), env.sem("summed"), env.sem("rooted"), env.sem("inverted")
        scaled, renewed, headed, split = (env.sem(n) for n in ("scaled", "renewed", "headed", "split"))
        stored = [env.sem(f"stored{k}") for k in range(2)]
        rounds = 1 if final else 2
        with nc.Block() as block:
            @block.sync
            def _(sp):
                for c in range(NB):
                    if c >= 2:
                        sp.wait_ge(stored[c % 2], 16 * (c // 2))
                        sp.wait_ge(scaled, KD * rounds * (c - 1))
                    sp.dma_start(x[c % 2][:, :, :], x_dram.rearrange("k p t -> p k t")[:, :, TB * c:TB * c + TB]).then_inc(x_in[c % 2], 16)

            @block.gpsimd
            def _(pool):
                for c in range(NB):
                    pool.wait_ge(renewed, KD * (c + 1))
                    if not final:
                        pool.dma_start(x_dram.rearrange("k p t -> p k t")[:, :, TB * c:TB * c + TB],
                                       x[c % 2][:, :, :]).then_inc(stored[c % 2], 16)
                    else:
                        pool.dma_start(y.rearrange("k p t -> p k t")[:, :, TB * c:TB * c + TB],
                                       x[c % 2][:, :, :]).then_inc(stored[c % 2], 16)
                pool.wait_ge(stored[0], 16 * 2)
                pool.wait_ge(stored[1], 16)

            @block.scalar
            def _(act):
                n = 0
                for c in range(NB):
                    for r in range(rounds):
                        for k in range(KD):
                            if n >= 4:
                                act.wait_ge(summed, n - 3)
                            if r == 1:
                                act.wait_ge(renewed, KD * c + k + 1)
                            src = f[:, k, TB * c:TB * c + TB] if r == 0 else x[c % 2][:, k, :]
                            act.activation(sq[n % 4][:, :], src, ACT.Square).then_inc(squared, 1)
                            n += 1
                        act.wait_ge(summed, n)
                        if n > KD:
                            act.wait_ge(inverted, n // KD - 1)
                        act.activation(root[:, :], bank[6 + (n // KD - 1) % 2][:, 0:TB], ACT.Sqrt, bias=env.eps,
                                       scale=1.0 / D).then_inc(rooted, 1)
                    if not final:
                        for k in range(KD):
                            act.wait_ge(scaled, KD * (2 * c + 1) + k + 1)
                            act.activation(h_head[:, k, TB * c:TB * c + TB], tmp[k % 4][:, :], ACT.Copy).then_inc(headed, 1)

            @block.tensor
            def _(pe):
                for n in range(NB * rounds * KD):
                    pe.wait_ge(squared, n + 1)
                    g = n // KD
                    if g >= 2 and n % KD == 0:
                        pe.wait_ge(rooted, g - 1)
                    pe.matmul(bank[6 + g % 2][:, 0:TB], env.ones[:, :], sq[n % 4][:, :], start=(n % KD == 0),
                              stop=(n % KD == KD - 1)).then_inc(summed, 1)

            @block.vector
            def _(dve):
                for c in range(NB):
                    cols = slice(TB * c, TB * c + TB)
                    for r in range(rounds):
                        g = rounds * c + r
                        dve.wait_ge(rooted, g + 1)
                        dve.reciprocal(inv[g % 2][:, :], root[:, :]).then_inc(inverted, 1)
                        dve.wait_ge(inverted, g + 1)
                        if r == 0:
                            dve.wait_ge(x_in[c % 2], 16 * (c // 2 + 1))
                        gain = env.gains[:, :, post if r == 0 else pre]

                        def second(k):
                            dve.wait_ge(scaled, KD * g + k + 1)
                            if r == 0:
                                dve.tensor_tensor(x[c % 2][:, k, :], x[c % 2][:, k, :], tmp[k % 4][:, :], ALU.add).then_inc(renewed, 1)
                            else:
                                dve.wait_ge(headed, KD * c + k + 1)
                                dve.tensor_tensor(h_rest[:, k, cols], tmp[k % 4][:, :], h_head[:, k, cols].bitcast(F32),
                                                  ALU.subtract).then_inc(split, 1)

                        for k in range(KD):
                            if k >= 2:
                                second(k - 2)
                            if k < 4 and g > 0:
                                if rounds == 1 or r == 1:
                                    dve.wait_ge(renewed, KD * (c + 1 if r == 1 else c))
                                else:
                                    dve.wait_ge(split, KD * c)
                            elif k >= 4:
                                if r == 0:
                                    dve.wait_ge(renewed, KD * c + k - 3)
                                else:
                                    dve.wait_ge(split, KD * c + k - 3)
                            src = f[:, k, cols] if r == 0 else x[c % 2][:, k, :]
                            dve.scalar_tensor_tensor(out=tmp[k % 4][:, :], in0=src, scalar=gain[:, k:k + 1],
                                                     in1=inv[g % 2][:, :], op0=ALU.mult, op1=ALU.mult).then_inc(scaled, 1)
                        second(KD - 2)
                        second(KD - 1)


UW = (FTAPS - 1) + SEQ + STREAMS * (FTAPS - 1 + STEPS)


def halo_views(u, taps, width):
    head = taps - 1
    return u[:, 0:head + SEQ], u[:, head + SEQ:width].rearrange("p (s t) -> p s t", s=STREAMS)


def params_in(env, dst, loads, tiles, rows):
    nc, bank = env.nc, env.bank
    per = 512 // rows
    with ExitStack() as scope:
        env.scope = scope
        stack = env.sb("stack", [rows, tiles * P])
        landed, turned, done = env.sem("landed"), env.sem("turned"), env.sem("done")
        batches = [(t, min(per, tiles - t)) for t in range(0, tiles, per)]
        with nc.Block() as block:
            @block.sync
            def _(sp):
                r = 0
                for src in loads:
                    sp.dma_start(stack[r:r + src.shape[0], :], src).then_inc(landed, 16)
                    r += src.shape[0]

            @block.tensor
            def _(pe):
                pe.wait_ge(landed, 16 * len(loads))
                for b, (t0, n) in enumerate(batches):
                    if b >= 2:
                        pe.wait_ge(done, b - 1)
                    for k in range(n):
                        m = pe.transpose(bank[b % 2][:, rows * k:rows * k + rows],
                                         stack[:, P * (t0 + k):P * (t0 + k) + P], env.ident[0:rows, 0:rows])
                    m.then_inc(turned, 1)

            @block.vector
            def _(dve):
                for b, (t0, n) in enumerate(batches):
                    dve.wait_ge(turned, b + 1)
                    dve.tensor_copy(dst[:, t0:t0 + n, :].rearrange("p t r -> p (t r)"),
                                    bank[b % 2][:, 0:rows * n]).then_inc(done, 1)


def rows_out(env, src, stores, tiles, rows):
    nc, bank = env.nc, env.bank
    with ExitStack() as scope:
        env.scope = scope
        stack = env.sb("stack", [rows, tiles * P])
        turned, done, stored = env.sem("turned"), env.sem("done"), env.sem("stored")
        NBAT = tiles // 4
        with nc.Block() as block:
            @block.tensor
            def _(pe):
                for b in range(NBAT):
                    if b >= 4:
                        pe.wait_ge(done, b - 3)
                    for k in range(4):
                        m = pe.transpose(bank[b % 4][0:rows, P * k:P * k + P], src[:, 4 * b + k, :], env.ident[:, :])
                    m.then_inc(turned, 1)

            @block.vector
            def _(dve):
                for b in range(NBAT):
                    dve.wait_ge(turned, b + 1)
                    dve.tensor_copy(stack[:, 4 * P * b:4 * P * b + 4 * P], bank[b % 4][0:rows, :]).then_inc(done, 1)

            @block.sync
            def _(sp):
                sp.wait_ge(done, NBAT)
                for dst, r in stores:
                    sp.dma_start(dst, stack[r:r + dst.shape[0], :]).then_inc(stored, 16)
                sp.wait_ge(stored, 16 * len(stores))


def ffn(env, w_up, w_down, par, tails, x_head, x_rest, f):
    nc, w, banks = env.nc, env.w, [env.bank[0:NB], env.bank[NB:2 * NB]]
    n0 = env.units
    H = FTAPS - 1
    TAP, BIAS = STREAMS * H, STREAMS * H + FTAPS
    up_src = w_up.rearrange("(k p) m -> p k m", p=P)
    down_src = w_down.rearrange("(t p) m -> p t m", p=P)
    with ExitStack() as scope:
        env.scope = scope
        u = [env.sb(f"u{k}", [P, UW]) for k in range(2)]
        cv = [env.sb(f"cv{k}", [P, T]) for k in range(2)]
        a_head = [env.sb(f"a_head{k}", [P, 2, T], F32R) for k in range(2)]
        a_rest = [env.sb(f"a_rest{k}", [P, 2, T], F32R) for k in range(2)]
        ready, halo, evac, saved, conved = (env.sem(n) for n in ("ready", "halo", "evac", "saved", "conved"))
        gelued, acted, headed, rested = (env.sem(n) for n in ("gelued", "acted", "headed", "rested"))
        down, added, tap = env.sem("down"), env.sem("added"), env.sem("tap")
        seq = [halo_views(u[k], FTAPS, UW) for k in range(2)]

        def tile_of(b, k):
            return b * 2 + (k // 2 + FT * (k % 2))

        def at(ap, tile, lo, hi):
            return ap[:, tile, lo:hi] if isinstance(tile, int) else \
                ap[:, bass.ds(tile, 1), lo:hi].rearrange("p o r -> p (o r)")

        def blocks(eng, body):
            body(0, 0, n0)
            body(1, 1, n0 + 4)
            with eng.Fori(1, FBLOCKS // 2) as i:
                for h in range(2):
                    body(i * 2 + h, h, i * 12 + (n0 - 2 + 6 * h))
            body(FBLOCKS - 1, (FBLOCKS - 1) % 2, n0 + 6 * (FBLOCKS - 1) - 2)

        last = n0 + 6 * FBLOCKS - 2
        env.units = last + 2
        with nc.Block() as block:
            @block.sync
            def _(sp):
                def body(b, _, n):
                    for k in range(4):
                        t = tile_of(b, k)
                        src = up_src[:, :, P * t:P * t + P] if isinstance(t, int) else up_src[:, :, bass.ds(t * P, P)]
                        w.load(sp, n + k, k % 2, src, first=isinstance(n, int) and n + k < 2)
                    if not isinstance(b, int) or b:
                        downs(b - 1, n + 4)

                def downs(b, n):
                    for h in range(2):
                        rows = down_src[:, 2 * b:2 * b + 2, :] if isinstance(b, int) else down_src[:, bass.ds(b * 2, 2), :]
                        w.load(sp, n + h, h, rows[:, :, 4 * P * h:4 * P * h + 4 * P])

                blocks(sp, body)
                downs(FBLOCKS - 1, last)

            @block.gpsimd
            def _(pool):
                for k in range(2):
                    pool.memset(u[k][:, 0:H], 0.0).then_inc(ready, 1)
                pool.memset(f[:, :, :], 0.0).then_inc(ready, 1)

                def body(b, _, n):
                    for k in range(4):
                        t = tile_of(b, k)
                        if not isinstance(b, int) or 4 * b + k >= 2:
                            pool.wait_ge(conved, b * 4 + (k - 1))
                        pool.tensor_copy(seq[k % 2][1][:, :, 0:H], at(par, t, 0, STREAMS * H).rearrange(
                            "p (s h) -> p s h", h=H)).then_inc(halo, 1)
                        pool.wait_ge(evac, b * 4 + (k + 1))
                        pool.tensor_copy(at(tails, t, 0, STREAMS * H).rearrange("p (s h) -> p s h", h=H),
                                         seq[k % 2][1][:, :, STEPS:])
                        pool.tensor_copy(at(tails, t, STREAMS * H, STREAMS * H + H), u[k % 2][:, SEQ:SEQ + H]).then_inc(saved, 1)

                blocks(pool, body)

            @block.tensor
            def _(pe):
                def body(b, par_, n):
                    later = not isinstance(b, int) or b
                    for k in range(4):
                        if k >= 2:
                            pe.wait_ge(evac, b * 4 + (k - 1))
                        elif not isinstance(b, int) or b >= 2:
                            pe.wait_ge(added, b * 8 - 8)
                        elif b:
                            pe.wait_ge(evac, b * 4 + (k - 1))
                        up_tile(pe, env, n + k, k % 2, x_head, x_rest, banks[k % 2])
                    if later:
                        pe.wait_ge(evac, b * 4 + 3)
                        downs(b - 1, 1 - par_, n + 4, b * 4 + 4)

                def downs(b, s, n, evacs):
                    pe.wait_ge(headed, b * 2 + 2)
                    pe.wait_ge(rested, b * 2 + 2)
                    for m in range(KD):
                        if m % 4 == 0:
                            w.ready(pe, n + m // 4)
                        if m == 1 and evacs is not None:
                            pe.wait_ge(evac, evacs)
                        if m >= 2 or evacs is None:
                            pe.wait_ge(added, b * 8 + (m - 1))
                        for k in range(2):
                            cols = slice(4 * P * k + P * (m % 4), 4 * P * k + P * (m % 4) + P)
                            for lhs, rhs, q in ((w.head, a_head, 0), (w.head, a_rest, 1), (w.rest, a_head, 2)):
                                for c in range(NB):
                                    ins = pe.matmul(banks[m % 2][c][:, 0:TB], lhs[m // 4][:, cols],
                                                    rhs[s][:, k, TB * c:TB * c + TB], start=(k == 0 and q == 0),
                                                    stop=(k == 1 and q == 2))
                        ins.then_inc(w.used if m % 4 == 3 else down, 1)

                blocks(pe, body)
                downs(FBLOCKS - 1, (FBLOCKS - 1) % 2, last, None)

            @block.scalar
            def _(act):
                w.round(act, n0, 0, first=(n0 == 0))
                w.round(act, n0 + 1, 1, first=(n0 == 0))
                act.wait_ge(ready, 3)

                def body(b, p_, n):
                    start = isinstance(b, int) and b == 0
                    for k in range(4):
                        w.round(act, n + (k + 2), k % 2)
                        g, i = k % 2, k // 2
                        if not start or k >= 2:
                            act.wait_ge(conved, b * 4 + (k - 1))
                            act.wait_ge(saved, b * 4 + (k - 1))
                            act.wait_ge(acted if g == 0 else rested, b * 2 + i)
                        t = tile_of(b, k)
                        bk, (up, us_) = banks[g], seq[g]
                        for c in range(NB):
                            act.activation(cv[g][:, TB * c:TB * c + TB], bk[c][:, 0:TB], ACT.Identity,
                                           scale=at(par, t, TAP + H, TAP + H + 1), bias=at(par, t, BIAS, BIAS + 1))
                        for c in range(NB):
                            n_p = min(TB, SEQ - TB * c)
                            act.activation(up[:, H + TB * c:H + TB * c + n_p], bk[c][:, 0:n_p], ACT.Copy)
                        act.activation(us_[:, :, H:], bk[NB - 1][:, SEQ - TB * (NB - 1):TB].rearrange(
                            "p (s t) -> p s t", s=STREAMS), ACT.Copy).then_inc(evac, 1)
                        if g == 1:
                            act.wait_ge(conved, b * 4 + k)
                            act.activation(cv[0][:, :], cv[0][:, :], ACT.Gelu_apprx_tanh).then_inc(gelued, 1)
                            act.wait_ge(acted, b * 2 + (i + 1))
                            if not isinstance(b, int) or b >= 2:
                                act.wait_ge(w.used, n)
                            act.activation(a_head[p_][:, i, :], cv[1][:, :], ACT.Copy).then_inc(headed, 1)
                    if not start:
                        for h in range(2):
                            w.round(act, n + (6 + h), h)

                blocks(act, body)

            @block.vector
            def _(dve):
                w.subtract(dve, n0, 0)
                w.subtract(dve, n0 + 1, 1)
                dve.wait_ge(ready, 3)

                def body(b, p_, n):
                    start = isinstance(b, int) and b == 0
                    for k in range(4):
                        w.subtract(dve, n + (k + 2), k % 2)
                        g, i, t = k % 2, k // 2, tile_of(b, k)
                        dve.wait_ge(halo, b * 4 + (k + 1))
                        dve.wait_ge(evac, b * 4 + (k + 1))
                        up, us_ = seq[g]
                        cp, cs = cv[g][:, 0:SEQ], cv[g][:, SEQ:].rearrange("p (s t) -> p s t", s=STREAMS)
                        for j in range(H):
                            tw = at(par, t, TAP + j, TAP + j + 1)
                            if j:
                                dve.wait_ge(tap, b * 8 + (2 * k + 1)) 
                            ins = dve.scalar_tensor_tensor(out=cp, in0=up[:, j:j + SEQ], scalar=tw, in1=cp, op0=ALU.mult, op1=ALU.add)
                            if j:
                                dve.wait_ge(tap, b * 8 + (2 * k + 2))
                            else:
                                ins.then_inc(tap, 1)
                            ins = dve.scalar_tensor_tensor(out=cs, in0=us_[:, :, j:j + STEPS], scalar=tw, in1=cs, op0=ALU.mult, op1=ALU.add)
                            ins.then_inc(tap if j == 0 else conved, 1)
                        if g == 1:
                            dve.wait_ge(gelued, b * 2 + (i + 1))
                            dve.wait_ge(conved, b * 4 + (k + 1))
                            dve.tensor_tensor(cv[1][:, :], cv[1][:, :], cv[0][:, :], ALU.mult).then_inc(acted, 1)
                            dve.wait_ge(headed, b * 2 + (i + 1))
                            dve.tensor_tensor(a_rest[p_][:, i, :], cv[1][:, :], a_head[p_][:, i, :].bitcast(F32),
                                              ALU.subtract).then_inc(rested, 1)
                    if not start:
                        adds(b - 1, n + 4, True)

                def adds(b, n, more):
                    for m in range(KD):
                        if m % 4 == 3:
                            dve.wait_ge(w.used, n + (m // 4 + 1))
                        else:
                            dve.wait_ge(down, b * 6 + (m + 1 - m // 4))
                        for c in range(NB):
                            ins = dve.tensor_tensor(f[:, m, TB * c:TB * c + TB], f[:, m, TB * c:TB * c + TB],
                                                    banks[m % 2][c][:, 0:TB], ALU.add)
                        ins.then_inc(added, 1)
                        if m % 4 == 3 and more:
                            w.subtract(dve, n + (2 + m // 4), m // 4)

                blocks(dve, body)
                adds(FBLOCKS - 1, last, False)


UM = (MTAPS - 1) + SEQ + STREAMS * (MTAPS - 1 + STEPS)
MH = MTAPS - 1
M_TAP, M_BIAS, M_GAIN, M_SKIP, M_ROWS = STREAMS * MH, STREAMS * MH + MTAPS, STREAMS * MH + MTAPS + 1, \
    STREAMS * MH + MTAPS + 2, STREAMS * MH + MTAPS + 3


def dyn(ap, index, lo=None, hi=None):
    tail = slice(lo, hi)
    return ap[:, index, tail] if isinstance(index, int) else ap[:, bass.ds(index, 1), tail].rearrange("p o r -> p (o r)")


def headwise_weights(env, wq, wk, wv, w_gate, bd, gate_w):
    nc = env.nc
    NBK = P // QB
    with ExitStack() as scope:
        env.scope = scope
        c = env.sb("c", [P, 3, IT, QB])
        g4 = env.sb("g4", [P, 3, IT, QB, 2 * HEADS])
        mask = env.sb("mask", [P, NBK])
        t = env.sb("t", [P, IT, 2 * HEADS])
        made, landed, done = env.sem("made"), env.sem("landed"), env.sem("done")
        with nc.Block() as block:
            @block.sync
            def _(sp):
                for k, wt in enumerate((wq, wk, wv)):
                    sp.dma_start(c[:, k, :, :], wt[0].rearrange("(j n) c d -> (n c) j d", j=IT)).then_inc(landed, 16)

            @block.scalar
            def _(act):
                for k in range(3):
                    src = w_gate[0, INNER * k:INNER * k + INNER, :].rearrange("(j n d) g -> n j (d g)", j=IT, d=QB)
                    for i in range(QB):
                        act.dma_start(g4[i:P:QB, k, :, :, :].rearrange("p j d g -> p j (d g)"), src).then_inc(landed, 16)

            @block.gpsimd
            def _(pool):
                pool.memset(mask[:, :], 1.0).then_inc(made, 1)
                pool.wait_ge(made, 1)
                pool.affine_select(out=mask[:, :], in_=mask[:, :], compare_op=ALU.is_ge, fill=0.0, base=0,
                                   pattern=[[-QB, NBK]], channel_multiplier=1).then_inc(made, 1)
                pool.wait_ge(made, 2)
                pool.affine_select(out=mask[:, :], in_=mask[:, :], compare_op=ALU.is_ge, fill=0.0, base=QB - 1,
                                   pattern=[[QB, NBK]], channel_multiplier=-1).then_inc(made, 1)

            @block.vector
            def _(dve):
                link = Link(dve, env.sem("link"))
                dve.wait_ge(landed, 16 * (3 + 3 * QB))
                dve.wait_ge(made, 3)
                for k in range(3):
                    dst = gate_w[:, :, 0:2 * HEADS] if k < 2 else gate_w[:, :, 2 * HEADS:]
                    for d in range(QB):
                        factor = bcast(c[:, k, :, d], 2, 2 * HEADS)
                        if d == 0 and k != 1:
                            link(dve.tensor_tensor(dst, g4[:, k, :, d, :], factor, ALU.mult))
                        else:
                            link(dve.tensor_tensor(t[:, :, :], g4[:, k, :, d, :], factor, ALU.mult))
                            link(dve.tensor_tensor(dst, dst, t[:, :, :], ALU.add))
                link(dve.tensor_scalar(c[:, 1, :, :], c[:, 1, :, :], float(DH) ** -0.5, None, ALU.mult))
                for k in range(3):
                    link(dve.tensor_tensor(bd[:, k, :, :].rearrange("p j (n d) -> p j n d", d=QB),
                                           bcast(c[:, k, :, :], 2, NBK), bcast(bcast(mask[:, :], 2, QB), 1, IT), ALU.mult))


def mlstm_up(env, w_up, par, tails, gate_w, b_gate, x_head, x_rest, xm_d, xc_d, sz_d, gates):
    nc, w, banks = env.nc, env.w, [env.bank[0:NB], env.bank[NB:2 * NB]]
    n0 = env.units
    env.units = n0 + 2 * IT
    src = w_up[0].rearrange("(k p) m -> p k m", p=P)
    with ExitStack() as scope:
        env.scope = scope
        u = env.sb("u", [P, UM])
        xm = [env.sb(f"xm{k}", [P, T]) for k in range(2)]
        xc = [env.sb(f"xc{k}", [P, T]) for k in range(2)]
        sz = [env.sb(f"sz{k}", [P, T]) for k in range(2)]
        gs = [env.sb(f"gs{k}", [P, 4 * HEADS]) for k in range(2)]
        bg = env.sb("bg", [2 * HEADS, 1])
        ready, evac, filled, conved, silued, zed, gated, tap, all_in, bias_in = (env.sem(n) for n in (
            "ready", "evac", "filled", "conved", "silued", "zed", "gated", "tap", "all_in", "bias_in"))
        copied = env.sem("copied")
        x_out = [env.sem(f"x_out{k}") for k in range(2)]
        z_out = [env.sem(f"z_out{k}") for k in range(2)]
        up, us_ = halo_views(u, MTAPS, UM)
        streams = lambda a: a.rearrange("p (s t) -> p s t", s=STREAMS)
        acc = [env.bank[6][0:2 * HEADS, 0:TB], env.bank[7][0:2 * HEADS, 0:TB], env.bank[6][32:32 + 2 * HEADS, 0:TB]]

        def tiles(eng, body):
            for j in range(2):
                body(j, j, n0 + 2 * j, j == 0, False)
            with eng.Fori(1, IT // 2 - 1) as i:
                for h in range(2):
                    body(i * 2 + h, h, i * 4 + (n0 + 2 * h), False, False)
            for j in range(IT - 2, IT):
                body(j, j % 2, n0 + 2 * j, False, j == IT - 1)

        def past(j, n):
            return not isinstance(j, int) or j >= n

        with nc.Block() as block:
            @block.sync
            def _(sp):
                def store(dst, s, sem, out, j, p_):
                    sp.wait_ge(sem, j + 1)
                    held(sp, w.freed)
                    sp.dma_start(dst[j] if isinstance(j, int) else dst[bass.ds(j, 1)].rearrange("o p t -> (o p) t"),
                                 s[p_][:, :]).then_inc(out[p_], 16)

                def body(j, p_, n, first, last):
                    for h in range(2):
                        col = P * j + INNER * h if isinstance(j, int) else bass.ds(j * P + INNER * h, P)
                        w.load(sp, n + h, h, src[:, :, col:col + P] if isinstance(j, int) else src[:, :, col],
                               first=isinstance(n, int) and n + h < 2)
                        if past(j, 2) and h == 0:
                            store(xm_d, xm, evac, x_out, j - 2, p_)
                            store(xc_d, xc, silued, x_out, j - 2, p_)
                        elif past(j, 2):
                            store(sz_d, sz, zed, z_out, j - 2, p_)
                tiles(sp, body)
                for j in range(IT - 2, IT):
                    store(xm_d, xm, evac, x_out, j, j % 2)
                    store(xc_d, xc, silued, x_out, j, j % 2)
                    store(sz_d, sz, zed, z_out, j, j % 2)
                for k in range(2):
                    sp.wait_ge(x_out[k], 16 * IT)
                    sp.wait_ge(z_out[k], 8 * IT)

            @block.gpsimd
            def _(pool):
                pool.dma_start(bg[:, :], b_gate[0].rearrange("(g o) -> g o", o=1)).then_inc(bias_in, 16)
                pool.memset(u[:, 0:MH], 0.0).then_inc(ready, 1)

                def body(j, p_, n, first, last):
                    if past(j, 1):
                        pool.wait_ge(conved, j)
                    if past(j, 2):
                        pool.wait_ge(gated, j - 1)
                    pool.tensor_copy(gs[p_][:, :], dyn(gate_w, j))
                    pool.tensor_copy(us_[:, :, 0:MH], dyn(par, j, 0, STREAMS * MH).rearrange("p (s h) -> p s h", h=MH))
                    pool.wait_ge(evac, j + 1)
                    held(pool, copied)
                    pool.tensor_copy(up[:, MH:], xm[p_][:, 0:SEQ])
                    pool.tensor_copy(us_[:, :, MH:], streams(xm[p_][:, SEQ:]))
                    pool.tensor_copy(dyn(tails, j, 0, STREAMS * MH).rearrange("p (s h) -> p s h", h=MH),
                                     streams(xm[p_][:, SEQ:])[:, :, STEPS - MH:])
                    pool.tensor_copy(dyn(tails, j, STREAMS * MH, STREAMS * MH + MH), xm[p_][:, SEQ - MH:SEQ]).then_inc(filled, 1)
                tiles(pool, body)

            @block.tensor
            def _(pe):
                def body(j, p_, n, first, last):
                    if past(j, 1):
                        pe.wait_ge(evac, j)
                    up_tile(pe, env, n, 0, x_head, x_rest, banks[0])
                    if past(j, 1):
                        pe.wait_ge(zed, j)
                    up_tile(pe, env, n + 1, 1, x_head, x_rest, banks[1])
                    pe.wait_ge(filled, j + 1)
                    pe.wait_ge(silued, j + 1)
                    for k, x in ((0, xc), (1, xm)):
                        for c in range(NB):
                            ins = pe.matmul(acc[c], gs[p_][:, 2 * HEADS * k:2 * HEADS * k + 2 * HEADS],
                                            x[p_][:, TB * c:TB * c + TB], start=(first and k == 0), stop=(last and k == 1),
                                            skip_group_check=True)
                    ins.then_inc(gated, 1)
                tiles(pe, body)

            @block.scalar
            def _(act):
                w.round(act, n0, 0, first=(n0 == 0))
                w.round(act, n0 + 1, 1, first=(n0 == 0))

                def body(j, p_, n, first, last):
                    act.wait_ge(w.used, n + 1)
                    if not last:
                        w.round(act, n + 2, 0)
                    if past(j, 2):
                        act.wait_ge(gated, j - 1)
                        act.wait_ge(x_out[p_], j * 16 - 16 * p_)
                    for c in range(NB):
                        act.activation(xm[p_][:, TB * c:TB * c + TB], banks[0][c][:, 0:TB], ACT.Copy)
                    for c in range(NB):
                        ins = act.activation(xc[p_][:, TB * c:TB * c + TB], banks[0][c][:, 0:TB], ACT.Identity,
                                             scale=dyn(par, j, M_TAP + MH, M_TAP + MH + 1),
                                             bias=dyn(par, j, M_BIAS, M_BIAS + 1))
                    ins.then_inc(evac, 1)
                    act.wait_ge(conved, j + 1)
                    act.activation(xc[p_][:, :], xc[p_][:, :], ACT.Silu).then_inc(silued, 1)
                    act.wait_ge(w.used, n + 2)
                    if not last:
                        w.round(act, n + 3, 1)
                    if past(j, 2):
                        act.wait_ge(z_out[p_], j * 8 - 8 * p_)
                    for c in range(NB):
                        ins = act.activation(sz[p_][:, TB * c:TB * c + TB], banks[1][c][:, 0:TB], ACT.Silu)
                    ins.then_inc(zed, 1)
                tiles(act, body)

            @block.vector
            def _(dve):
                w.subtract(dve, n0, 0)
                w.subtract(dve, n0 + 1, 1)
                dve.wait_ge(ready, 1)

                def body(j, p_, n, first, last):
                    if not last:
                        w.subtract(dve, n + 2, 0)
                    dve.wait_ge(filled, j + 1)
                    cp, cs = xc[p_][:, 0:SEQ], streams(xc[p_][:, SEQ:])
                    for i in range(MH):
                        tw = dyn(par, j, M_TAP + i, M_TAP + i + 1)
                        if i:
                            dve.wait_ge(tap, j * (2 * MH) + (2 * i))
                        dve.scalar_tensor_tensor(out=cp, in0=up[:, i:i + SEQ], scalar=tw, in1=cp, op0=ALU.mult,
                                                 op1=ALU.add).then_inc(tap, 1)
                        dve.scalar_tensor_tensor(out=cs, in0=us_[:, :, i:i + STEPS], scalar=tw, in1=cs, op0=ALU.mult,
                                                 op1=ALU.add).then_inc(tap, 1)
                    dve.wait_ge(tap, j * (2 * MH) + 2 * MH)
                    dve.sem_inc(conved, 1)
                    if not last:
                        w.subtract(dve, n + 3, 1)
                tiles(dve, body)
                dve.wait_ge(gated, IT)
                dve.wait_ge(bias_in, 16)
                for c in range(NB):
                    dve.tensor_scalar(gates[:, TB * c:TB * c + TB], acc[c], bg[:, :], None, ALU.add).then_inc(all_in, 1)


def gate_rows(env, gates, m_in, rows, cols, m_out_p, m_out_s):
    nc, bank = env.nc, env.bank
    H = HEADS
    with ExitStack() as scope:
        env.scope = scope
        ig, lf, b, m, t0, t1, t2, keep = (env.sb(n, [H, T]) for n in ("ig", "lf", "b", "m", "t0", "t1", "t2", "keep"))
        m0 = env.sb("m0", [H, STREAMS])
        landed, picked, sums, logs, exps, turned, stored, seeds = (env.sem(n) for n in (
            "landed", "picked", "sums", "logs", "exps", "turned", "stored", "seeds"))
        streams = lambda a: a[:, SEQ:].rearrange("h (s t) -> h s t", s=STREAMS)
        chunks = lambda a: a[:, 0:SEQ].rearrange("h (c t) -> h c t", t=P)
        with nc.Block() as block:
            @block.sync
            def _(sp):
                sp.dma_start(m0[:, :], m_in[0].rearrange("s h -> h s"), allow_slow_non_contiguous=True).then_inc(landed, 16)
                sp.wait_ge(seeds, 1)
                sp.dma_start(m_out_p[0].rearrange("o h -> h o"), m[:, SEQ - 1:SEQ], allow_slow_non_contiguous=True).then_inc(stored, 16)
                sp.dma_start(m_out_s[0].rearrange("s h -> h s"), streams(m)[:, :, STEPS - 1], allow_slow_non_contiguous=True).then_inc(stored, 16)
                sp.wait_ge(stored, 32)

            @block.tensor
            def _(pe):
                for k in range(2):
                    for c in range(NB):
                        ins = pe.matmul(bank[NB * k + c][0:H, 0:TB], env.ident[0:2 * H, H * k:H * k + H],
                                        gates[:, TB * c:TB * c + TB], start=True, stop=True)
                ins.then_inc(picked, 1)
                pe.wait_ge(sums, 1)
                for k, src in enumerate((t0, t1)):
                    if k:
                        pe.wait_ge(exps, 3)
                    for c in range(CHUNKS):
                        ins = pe.transpose(bank[6][:, H * (2 * c + k):H * (2 * c + k) + H], src[:, P * c:P * c + P],
                                           env.ident[0:H, 0:H])
                ins.then_inc(turned, 1)

            @block.scalar
            def _(act):
                act.wait_ge(logs, 1)
                act.activation(t0[:, :], lf[:, :], ACT.Abs).then_inc(exps, 1)
                act.wait_ge(exps, 1)
                act.activation(t0[:, :], t0[:, :], ACT.Exp, scale=-1.0).then_inc(exps, 1)
                act.wait_ge(logs, 2)
                act.activation(t2[:, :], t1[:, :], ACT.Ln).then_inc(logs, 1)
                act.wait_ge(sums, 1)
                act.activation(t1[:, :], m[:, :], ACT.Exp, scale=-1.0).then_inc(exps, 1)
                act.wait_ge(sums, 2)
                act.activation(rows[:, :, 1, :], rows[:, :, 1, :], ACT.Exp).then_inc(exps, 1)

            @block.vector
            def _(dve):
                link = Link(dve, env.sem("link"))
                tt, ts = dve.tensor_tensor, dve.tensor_scalar
                link(dve.memset(keep[:, :], 1.0))
                link(dve.memset(keep[:, 0:SEQ:P], 0.0))
                link(dve.memset(keep[:, SEQ:T:STEPS], 0.0))
                dve.wait_ge(picked, 1)
                for c in range(NB):
                    link(dve.tensor_copy(ig[:, TB * c:TB * c + TB], bank[c][0:H, 0:TB]))
                    ins = dve.tensor_copy(lf[:, TB * c:TB * c + TB], bank[NB + c][0:H, 0:TB])
                    if c < NB - 1:
                        link(ins)
                ins.then_inc(logs, 1)
                dve.wait_ge(exps, 2)
                ts(t1[:, :], t0[:, :], 1.0, None, ALU.add).then_inc(logs, 1)
                dve.wait_ge(logs, 3)
                link(dve.scalar_tensor_tensor(out=t0[:, :], in0=t1[:, :], scalar=-1.0, in1=t0[:, :], op0=ALU.add, op1=ALU.subtract))
                link(dve.reciprocal(t1[:, :], t1[:, :]))
                link(tt(t0[:, :], t0[:, :], t1[:, :], ALU.mult))
                link(tt(t2[:, :], t2[:, :], t0[:, :], ALU.subtract))
                link(dve.scalar_tensor_tensor(out=lf[:, :], in0=lf[:, :], scalar=0.0, in1=t2[:, :], op0=ALU.min, op1=ALU.subtract))
                link(dve.tensor_tensor_scan(b[:, :], keep[:, :], lf[:, :], 0.0, ALU.mult, ALU.add))
                link(dve.tensor_tensor_scan(m[:, 0:SEQ], lf[:, 0:SEQ], ig[:, 0:SEQ], 0.0, ALU.add, ALU.max))
                dve.wait_ge(landed, 16)
                for s in range(STREAMS):
                    cut = slice(SEQ + STEPS * s, SEQ + STEPS * s + STEPS)
                    link(dve.tensor_tensor_scan(m[:, cut], lf[:, cut], ig[:, cut], m0[:, s:s + 1], ALU.add, ALU.max))
                link(tt(t0[:, :], ig[:, :], b[:, :], ALU.subtract))
                link(tt(b[:, :], b[:, :], m[:, :], ALU.subtract))
                dve.sem_inc(sums, 1)
                dve.sem_inc(seeds, 1)
                r0, r1 = rows[:, :, 0, :], rows[:, :, 1, :]
                link(dve.tensor_copy(r0, b[:, :].rearrange("h (c t) -> h c t", t=P)))
                link(dve.tensor_copy(r1[:, 0, :], b[:, 0:P]))
                link(tt(r1[:, 1:PCH, :], chunks(b)[:, 1:, :], bcast(m[:, P - 1:SEQ - P:P], 2, P), ALU.add))
                link(tt(r1[:, PCH, :].rearrange("h (s t) -> h s t", s=STREAMS), streams(b), bcast(m0[:, :], 2, STEPS), ALU.add))
                dve.sem_inc(sums, 1)
                dve.wait_ge(turned, 1)
                link(dve.tensor_copy(cols[:, :, :, :].rearrange("p c k h -> p (c k h)"), bank[6][:, 0:2 * H * CHUNKS]))


class Cell:

    def __init__(self, env, bd):
        self.bd = bd
        two = lambda n, shape: [env.sb(f"{n}{k}", shape) for k in range(2)]
        self.xc, self.xm, self.sz = (two(n, [P, HT, P]) for n in ("c_xc", "c_xm", "c_sz"))
        self.q, self.k, self.qa, self.v, self.kw = (two(n, [P, HT, P]) for n in ("c_q", "c_k", "c_qa", "c_v", "c_kw"))
        self.e, self.em, self.sc = (two(n, [P, P]) for n in ("c_e", "c_em", "c_sc"))
        self.h, self.hn, self.t1, self.t2 = (two(n, [P, HT, P]) for n in ("c_h", "c_hn", "c_t1", "c_t2"))
        self.stats, self.mv, self.small = two("c_stats", [P, 6]), two("c_mv", [P, 2]), two("c_small", [P, 4])

    def project(self, pe, env, h, s):
        bank, bd = env.bank, self.bd
        for n, (w, x) in enumerate(((0, self.xc), (1, self.xc))):
            for t in range(HT):
                pe.matmul(bank[n][:, P * t:P * t + P], bd[:, w, HT * h + t, :], x[s][:, t, :], start=True, stop=True)
        for n, (w, x) in enumerate(((1, self.xc), (2, self.xm))):
            for t in range(HT):
                ins = pe.matmul(bank[2 + n][:, P * t:P * t + P], x[s][:, t, :], bd[:, w, HT * h + t, :], start=True, stop=True)
        return ins


def flat(a):
    return a[:, :, :].rearrange("p a b -> p (a b)")


def four(a):
    return a.rearrange("p (a b) -> p a b", a=HT)


def memories(space, n):
    s = space[:, :, :].rearrange("p k t -> p (k t)")
    return [s[:, HT * DH * h:HT * DH * h + HT * DH].rearrange("p (a b) -> p a b", a=HT) for h in range(n)]


def cell_masks(env, tri, tri_s, last_s, member):
    nc = env.nc
    made = env.sem("made")
    env.sel = env.sb("sel", [HEADS, HEADS, P])
    env.minus_half = env.sb("minus_half", [P, 1])
    with nc.Block() as block:
        @block.gpsimd
        def _(pool):
            n = 0
            def step(ins):
                nonlocal n
                n += 1
                ins.then_inc(made, 1)
                pool.wait_ge(made, n)
            def cut(a, op, base, pattern, mult):
                step(pool.affine_select(out=a, in_=a, compare_op=op, fill=0.0, base=base, pattern=pattern, channel_multiplier=mult))
            for a in (tri[:, :], tri_s[:, :], last_s[:, :], member[:, :], env.sel[:, :, :]):
                step(pool.memset(a, 1.0))
            step(pool.memset(env.minus_half[:, :], -0.5))
            cut(tri[:, :], ALU.is_ge, 0, [[1, P]], -1)
            cut(tri_s[:, :], ALU.is_ge, 0, [[1, P]], -1)
            by_stream = lambda a: a[:, :].rearrange("p (s t) -> p s t", s=STREAMS)
            for a in (tri_s, last_s):
                cut(by_stream(a), ALU.is_ge, 0, [[-STEPS, STREAMS], [0, STEPS]], 1)
                cut(by_stream(a), ALU.is_ge, STEPS - 1, [[STEPS, STREAMS], [0, STEPS]], -1)
            cut(by_stream(last_s), ALU.is_equal, 1 - STEPS, [[0, STREAMS], [1, STEPS]], 0)
            cut(member[:, :], ALU.is_ge, 0, [[-STEPS, STREAMS]], 1)
            cut(member[:, :], ALU.is_ge, STEPS - 1, [[STEPS, STREAMS]], -1)
            cut(env.sel[:, :, :], ALU.is_equal, 0, [[-1, HEADS], [0, P]], 1)


def mlstm_prompt(env, cell, par, rows, cols, tri, xm_d, xc_d, sz_d, hs, space, c_out, n_out):
    nc, bank = env.nc, env.bank
    with ExitStack() as scope:
        env.scope = scope
        ct = memories(space, HEADS)
        nt = env.sb("nt", [P, HEADS, HT])
        dec = env.sb("dec", [P, 2])
        x_in = [env.sem(f"x_in{k}") for k in range(2)]
        (projected, qk, vcopied, kwd, spread, d_bank4, exp_in, exped, masked, scored, weighted, numbered, den_read,
         rowed, updated, n_sum, n_done, normed, turned, joined, scaled, finished, ready, powed, stat, small) = (
            env.sem(n) for n in (
                "projected", "qk", "vcopied", "kwd", "spread", "d_bank4", "exp_in", "exped", "masked", "scored", "weighted",
                "numbered", "den_read", "rowed", "updated", "n_sum", "n_done", "normed", "turned", "joined", "scaled",
                "finished", "ready", "powed", "stat", "small"))

        stat2, joined2, d_row, d_stat, bounded, dve_held, pe_held, sp_held = (env.sem(n) for n in (
            "stat2", "joined2", "d_row", "d_stat", "bounded", "dve_held", "pe_held", "sp_held"))

        def chunks(eng, body):
            body(0, 0)
            body(1, 1)
            with eng.Fori(1, PCH // 2) as k:
                for s in range(2):
                    body(k * 2 + s, s)

        def ge(eng, sem, c, h, times=1, plus=0):
            if isinstance(c, int):
                v = times * (HEADS * c + h) + plus
                if v > 0:
                    eng.wait_ge(sem, v)
            else:
                eng.wait_ge(sem, c * (times * HEADS) + (times * h + plus))

        def cut(c):
            return slice(P * c, P * c + P) if isinstance(c, int) else bass.ds(c * P, P)

        with nc.Block() as block:
            @block.sync
            def _(sp):
                def body(c, s):
                    for h in range(HEADS):
                        ge(sp, finished, c, h, 1, -1)
                        if not isinstance(c, int):
                            held(sp, sp_held)
                        for dst, src in ((cell.xc, xc_d), (cell.xm, xm_d), (cell.sz, sz_d)):
                            sp.dma_start(dst[h % 2][:, :, :], src.rearrange("k p t -> p k t")[:, HT * h:HT * h + HT, cut(c)]).then_inc(
                                x_in[h % 2], 16)
                chunks(sp, body)

            @block.tensor
            def _(pe):
                def project(c, h, s):
                    pe.wait_ge(x_in[h % 2], c * 96 + (48 * (h // 2) + 48))
                    ge(pe, qk, c, h)
                    ge(pe, kwd, c, h)
                    ge(pe, vcopied, c, h)
                    cell.project(pe, env, h, h % 2).then_inc(projected, 1)

                def body(c, s):
                    if s == 0:
                        project(c, 0, 0)
                    for h in range(HEADS):
                        y = h % 2
                        ge(pe, n_done, c, h)
                        held(pe, pe_held)
                        src = rows[:, c, :, :] if isinstance(c, int) else rows[:, bass.ds(c, 1), :, :].rearrange("h o k t -> h (o k) t")
                        pe.matmul(bank[4][:, 0:2 * P], env.sel[:, h, :], src.rearrange("h k t -> h (k t)"),
                                  start=True, stop=True).then_inc(spread, 1)
                        ge(pe, qk, c, h, 1, 1)
                        ge(pe, updated, c, h, 4)
                        for t in range(HT):
                            ins = pe.matmul(bank[5][:, 0:P], cell.k[y][:, t, :], cell.q[y][:, t, :], start=(t == 0), stop=(t == HT - 1))
                        ins.then_inc(scored, 1)
                        if h < HEADS - 1:
                            project(c, h + 1, s)
                        elif s == 0:
                            project(c + 1, 0, 1)
                        ge(pe, d_bank4, c, h, 1, 1)
                        ge(pe, weighted, c, h, 1, 1)
                        ge(pe, vcopied, c, h, 1, 1)
                        pe.wait_ge(ready, HEADS + 1)
                        pe.matmul(bank[4][:, 256:257], cell.sc[y][:, :], env.ones[:, 0:1], start=True, stop=False)
                        for t in range(HT):
                            pe.matmul(bank[4][:, 256:257], cell.qa[y][:, t, :], nt[:, h, t:t + 1], start=False, stop=(t == HT - 1))
                        ge(pe, joined, c, h)
                        pe.matmul(bank[6][:, :], cell.sc[y][:, :], flat(cell.v[y]), start=True, stop=False)
                        for t in range(HT):
                            ins = pe.matmul(bank[6][:, :], cell.qa[y][:, t, :], ct[h][:, t, :], start=False, stop=(t == HT - 1))
                        ins.then_inc(numbered, 1)
                        ge(pe, kwd, c, h, 1, 1)
                        ge(pe, den_read, c, h, 1, 1)
                        for t in range(HT):
                            ins = pe.matmul(bank[4][:, 260 + t:261 + t], cell.kw[y][:, t, :], env.ones[:, 0:1], start=True, stop=True)
                        ins.then_inc(n_sum, 1)
                        for t in range(HT):
                            if t == 1:
                                ge(pe, updated, c, h, 4)
                            elif t > 1:
                                ge(pe, updated, c, h, 4, t - 1)
                            pe.matmul(bank[5 + 2 * (t % 2)][:, :], cell.kw[y][:, t, :], flat(cell.v[y]), start=True,
                                      stop=True).then_inc(stat, 1)
                        ge(pe, normed, c, h, 1, 1)
                        for t in range(HT):
                            ins = pe.transpose(bank[6][:, P * t:P * t + P], cell.hn[y][:, t, :], env.ident[:, :])
                        ins.then_inc(turned, 1)
                chunks(pe, body)

            @block.scalar
            def _(act):
                def keys(c, h):
                    ge(act, projected, c, h, 1, 1)
                    y = h % 2
                    act.activation(flat(cell.q[y]), bank[0][:, :], ACT.Copy)
                    act.activation(flat(cell.k[y]), bank[1][:, :], ACT.Copy).then_inc(qk, 1)

                def body(c, s):
                    if s == 0:
                        keys(c, 0)
                    for h in range(HEADS):
                        y = h % 2
                        ge(act, exp_in, c, h, 1, 1)
                        act.activation(cell.e[y][:, :], cell.e[y][:, :], ACT.Exp).then_inc(exped, 1)
                        ge(act, exped, c, h, 1, 1)
                        act.activation(flat(cell.kw[y]), bank[2][:, :], ACT.Copy, scale=cell.e[y][:, P - 1:P]).then_inc(kwd, 1)
                        if h < HEADS - 1:
                            keys(c, h + 1)
                        elif s == 0:
                            keys(c + 1, 0)
                        ge(act, small, c, h, 1, 1)
                        ge(act, numbered, c, h, 1, 1)
                        act.activation(flat(cell.h[y]), bank[6][:, :], ACT.Copy, scale=cell.small[y][:, 1:2]).then_inc(rowed, 1)
                chunks(act, body)

            @block.gpsimd
            def _(pool):
                for h in range(HEADS):
                    pool.memset(ct[h][:, :, :], 0.0).then_inc(ready, 1)
                pool.memset(nt[:, :, :], 0.0).then_inc(ready, 1)

                def body(c, s):
                    for h in range(HEADS):
                        y, tiles = h % 2, slice(HT * h, HT * h + HT)
                        ge(pool, exped, c, h, 1, 1)
                        pool.tensor_tensor(cell.em[y][:, :], cell.e[y][:, :], tri[:, :], ALU.mult).then_inc(masked, 1)
                        ge(pool, joined, c, h, 1, -1)
                        pool.tensor_tensor(cell.t2[y][:, :, :], cell.xc[y][:, :, :],
                                           bcast(par[:, tiles, M_SKIP], 2, P), ALU.mult).then_inc(scaled, 1)
                        ge(pool, stat2, c, h, 1, 1)
                        pool.tensor_tensor(cell.small[y][:, 2:3], cell.small[y][:, 3:4], env.minus_half[:, :], ALU.pow).then_inc(powed, 1)
                        ge(pool, joined2, c, h, 1, 1)
                        pool.tensor_tensor(hs[:, tiles, cut(c)], cell.t1[y][:, :, :], cell.sz[y][:, :, :],
                                           ALU.mult).then_inc(finished, 1)
                chunks(pool, body)

            @block.vector
            def _(dve):
                def body(c, s):
                    for h in range(HEADS):
                        y = h % 2
                        ge(dve, projected, c, h, 1, 1)
                        dve.tensor_copy(flat(cell.v[y]), bank[3][:, :]).then_inc(vcopied, 1)
                        ge(dve, spread, c, h, 1, 1)
                        ib = cols[:, c, 0, h:h + 1] if isinstance(c, int) else cols[:, bass.ds(c, 1), 0, h:h + 1].rearrange("p o h -> p (o h)")
                        em = cols[:, c, 1, h:h + 1] if isinstance(c, int) else cols[:, bass.ds(c, 1), 1, h:h + 1].rearrange("p o h -> p (o h)")
                        dve.tensor_scalar(cell.e[y][:, :], bank[4][:, 0:P], ib, 0.0, ALU.add, ALU.min).then_inc(exp_in, 1)
                        dve.tensor_copy(dec[:, y:y + 1], bank[4][:, 2 * P - 1:2 * P])
                        ge(dve, qk, c, h, 1, 1)
                        dve.tensor_tensor(cell.qa[y][:, :, :], cell.q[y][:, :, :], bcast(bank[4][:, P:2 * P], 1, HT),
                                          ALU.mult).then_inc(d_bank4, 1)
                        ge(dve, masked, c, h, 1, 1)
                        ge(dve, scored, c, h, 1, 1)
                        dve.tensor_tensor(cell.sc[y][:, :], cell.em[y][:, :], bank[5][:, 0:P], ALU.mult).then_inc(weighted, 1)
                        ge(dve, numbered, c, h, 1, 1)
                        dve.tensor_scalar(cell.small[y][:, 0:1], bank[4][:, 256:257], em, None, ALU.max).then_inc(bounded, 1)
                        ge(dve, bounded, c, h, 1, 1)
                        dve.scalar_tensor_tensor(out=cell.small[y][:, 0:1], in0=bank[4][:, 256:257], scalar=-1.0,
                                                 in1=cell.small[y][:, 0:1], op0=ALU.mult, op1=ALU.max).then_inc(den_read, 1)
                        ge(dve, den_read, c, h, 1, 1)
                        dve.reciprocal(cell.small[y][:, 1:2], cell.small[y][:, 0:1]).then_inc(small, 1)

                        def memory(t):
                            ge(dve, stat, c, h, 4, t + 1)
                            if t == 0:
                                ge(dve, d_bank4, c, h, 1, 1)
                            dve.scalar_tensor_tensor(out=ct[h][:, t, :], in0=ct[h][:, t, :], scalar=dec[:, y:y + 1],
                                                     in1=bank[5 + 2 * (t % 2)][:, :], op0=ALU.mult, op1=ALU.add).then_inc(updated, 1)

                        memory(0)
                        ge(dve, rowed, c, h, 1, 1)
                        dve.bn_stats(cell.stats[y][:, :], flat(cell.h[y])).then_inc(d_row, 1)
                        memory(1)
                        ge(dve, d_row, c, h, 1, 1)
                        held(dve, dve_held)
                        dve.bn_aggr(cell.mv[y][:, :], cell.stats[y][:, :]).then_inc(d_stat, 1)
                        ge(dve, d_stat, c, h, 1, 1)
                        dve.tensor_scalar(cell.small[y][:, 3:4], cell.mv[y][:, 1:2], LN_EPS, None, ALU.add).then_inc(stat2, 1)
                        ge(dve, n_sum, c, h, 1, 1)
                        dve.scalar_tensor_tensor(out=nt[:, h, :], in0=nt[:, h, :], scalar=dec[:, y:y + 1],
                                                 in1=bank[4][:, 260:260 + HT], op0=ALU.mult, op1=ALU.add).then_inc(n_done, 1)
                        memory(2)
                        ge(dve, powed, c, h, 1, 1)
                        dve.tensor_scalar(flat(cell.hn[y]), flat(cell.h[y]), cell.mv[y][:, 0:1], cell.small[y][:, 2:3],
                                          ALU.subtract, ALU.mult).then_inc(normed, 1)
                        memory(3)
                        tiles = slice(HT * h, HT * h + HT)
                        ge(dve, turned, c, h, 1, 1)
                        ge(dve, finished, c, h, 1, -1)
                        dve.tensor_tensor(cell.t1[y][:, :, :], four(bank[6][:, :]), bcast(par[:, tiles, M_GAIN], 2, P),
                                          ALU.mult).then_inc(joined, 1)
                        ge(dve, joined, c, h, 1, 1)
                        ge(dve, scaled, c, h, 1, 1)
                        dve.tensor_tensor(flat(cell.t1[y]), flat(cell.t1[y]), flat(cell.t2[y]), ALU.add).then_inc(joined2, 1)
                chunks(dve, body)

        with ExitStack() as inner:
            env.scope = inner
            out = [flat(a) for a in (*cell.q, *cell.k)]
            nrow = flat(cell.v[0])[0:HEADS, :]
            t_c, e_c, s_n = env.sem("t_c"), env.sem("e_c"), env.sem("s_n")
            s_c = [env.sem(f"s_c{k}") for k in range(4)]
            with nc.Block() as block:
                @block.tensor
                def _(pe):
                    for h in range(HEADS):
                        for v in range(HT):
                            n = HT * h + v
                            if n >= 4:
                                pe.wait_ge(e_c, n - 3)
                            for k in range(HT):
                                ins = pe.transpose(bank[n % 4][:, P * k:P * k + P], ct[h][:, k, P * v:P * v + P], env.ident[:, :])
                            ins.then_inc(t_c, 1)
                    for k in range(HT):
                        ins = pe.transpose(bank[4][0:HEADS, P * k:P * k + P], nt[:, :, k], env.ident[:, :])
                    ins.then_inc(t_c, 1)

                @block.scalar
                def _(act):
                    for n in range(HEADS * HT):
                        act.wait_ge(t_c, n + 1)
                        if n >= 4:
                            act.wait_ge(s_c[n % 4], 16 * (n // 4))
                        act.activation(out[n % 4], bank[n % 4][:, :], ACT.Copy).then_inc(e_c, 1)
                    act.wait_ge(t_c, HEADS * HT + 1)
                    act.activation(nrow, bank[4][0:HEADS, :], ACT.Copy).then_inc(e_c, 1)

                @block.sync
                def _(sp):
                    for n in range(HEADS * HT):
                        sp.wait_ge(e_c, n + 1)
                        sp.dma_start(c_out[0, 0, n // HT, P * (n % HT):P * (n % HT) + P, :], out[n % 4]).then_inc(s_c[n % 4], 16)
                    sp.wait_ge(e_c, HEADS * HT + 1)
                    sp.dma_start(n_out[0, 0], nrow).then_inc(s_n, 16)
                    for k in range(4):
                        sp.wait_ge(s_c[k], 16 * HEADS)
                    sp.wait_ge(s_n, 16)


def mlstm_streams(env, cell, par, rows, cols, tri_s, last_s, member, xm_d, xc_d, sz_d, C_in, n_in, hs, space, c_out, n_out):
    nc, bank = env.nc, env.bank
    SR = STREAMS * HEADS
    last = slice(SEQ, T)
    with ExitStack() as scope:
        env.scope = scope
        *craw, more, rest = memories(space, 4)
        tiles = [m[:, a, :].rearrange("p (a b) -> p a b", a=HT) for m in (more, rest) for a in range(HT)]
        qa, kw, v = [*cell.qa, *tiles[0:2]], [*cell.kw, *tiles[2:4]], [*cell.v, *tiles[4:6]]
        sc = [*cell.sc, *(env.sb(f"sc{k}", [P, P]) for k in range(2))]
        inter_t = [*cell.q, *cell.k]
        kwm = [cell.t1[0], cell.t1[1]]
        adec = tiles[6]
        wg = env.sb("wg", [P, HEADS])
        nrow = env.sb("nrow", [SR, DH])
        nt, nn = env.sb("nt", [P, HT, SR]), env.sb("nn", [P, HT, HEADS, STREAMS])
        *cnew, cts = (cell.bd[:, k, :, :].rearrange("p (a b) c -> p a (b c)", a=HT) for k in range(3))
        by_stream = lambda a: a.rearrange("p (s t) -> p s t", s=STREAMS)

        def over(eng, sem, value):
            if not isinstance(value, int) or value > 0:
                eng.wait_ge(sem, value)

        x_in = [env.sem(f"x_in{k}") for k in range(2)]
        (nrow_in, n_turned, projected, qk, vcopied, kwd, spread, exp_in, exped, masked, lasts, summed, d_bank4, scored,
         weighted) = (env.sem(n) for n in (
             "nrow_in", "n_turned", "projected", "qk", "vcopied", "kwd", "spread", "exp_in", "exped", "masked", "lasts",
             "summed", "d_bank4", "scored", "weighted"))
        c_in = [env.sem(f"c_in{k}") for k in range(2)]

        def c_load(sp, p, s, h):
            src = C_in[0, s, h].rearrange("(t p) k -> p t k", p=P) if isinstance(s, int) else \
                C_in[0, bass.ds(s, 1), h].rearrange("o (t p) k -> p (o t) k", p=P)
            sp.dma_start(craw[p][:, :, :], src).then_inc(c_in[p], 16)

        with nc.Block() as block:
            @block.sync
            def _(sp):
                sp.dma_start(nrow[:, :], n_in[0].rearrange("s h k -> (s h) k")).then_inc(nrow_in, 16)
                for h in range(HEADS):
                    over(sp, projected, h - 1)
                    for dst, src in ((cell.xc, xc_d), (cell.xm, xm_d)):
                        sp.dma_start(dst[h % 2][:, :, :], src.rearrange("k p t -> p k t")[:, HT * h:HT * h + HT, last]).then_inc(
                            x_in[h % 2], 16)
                for p in range(2):
                    c_load(sp, p, p, 0)

            @block.tensor
            def _(pe):
                pe.wait_ge(nrow_in, 16)
                for k in range(HT):
                    ins = pe.transpose(bank[6][:, SR * k:SR * k + SR], nrow[:, P * k:P * k + P], env.ident[0:SR, 0:SR])
                ins.then_inc(n_turned, 1)
                for h in range(HEADS):
                    over(pe, d_bank4, h)
                    pe.matmul(bank[4][:, 0:2 * P], env.sel[:, h, :], rows[:, PCH, :, :].rearrange("h k t -> h (k t)"),
                              start=True, stop=True).then_inc(spread, 1)
                    pe.wait_ge(x_in[h % 2], 32 * (h // 2 + 1))
                    for sem in (qk, kwd, vcopied):
                        over(pe, sem, h)
                    cell.project(pe, env, h, h % 2).then_inc(projected, 1)
                    pe.wait_ge(qk, h + 1)
                    over(pe, weighted, h)
                    for t in range(HT):
                        ins = pe.matmul(bank[5][:, 0:P], cell.k[h % 2][:, t, :], cell.q[h % 2][:, t, :], start=(t == 0), stop=(t == HT - 1))
                    ins.then_inc(scored, 1)

            @block.scalar
            def _(act):
                for h in range(HEADS):
                    y = h % 2
                    act.wait_ge(projected, h + 1)
                    over(act, weighted, h - 1)
                    over(act, d_bank4, h - 1)
                    act.activation(flat(cell.q[y]), bank[0][:, :], ACT.Copy)
                    act.activation(flat(cell.k[y]), bank[1][:, :], ACT.Copy).then_inc(qk, 1)
                    act.wait_ge(exp_in, h + 1)
                    act.activation(cell.e[y][:, :], cell.e[y][:, :], ACT.Exp).then_inc(exped, 1)
                    act.wait_ge(summed, h + 1)
                    act.activation(flat(kw[h]), bank[2][:, :], ACT.Copy, scale=wg[:, h:h + 1]).then_inc(kwd, 1)

            @block.gpsimd
            def _(pool):
                for h in range(HEADS):
                    y = h % 2
                    pool.wait_ge(exped, h + 1)
                    over(pool, summed, h - 1)
                    pool.tensor_tensor(cell.h[y][:, 0, :], cell.e[y][:, :], last_s[:, :], ALU.mult).then_inc(lasts, 1)
                    over(pool, weighted, h - 1)
                    pool.tensor_tensor(cell.em[y][:, :], cell.e[y][:, :], tri_s[:, :], ALU.mult).then_inc(masked, 1)

            @block.vector
            def _(dve):
                dve.wait_ge(n_turned, 1)
                dve.tensor_copy(nt[:, :, :].rearrange("p k r -> p (k r)"), bank[6][:, 0:HT * SR])
                for h in range(HEADS):
                    y = h % 2
                    dve.wait_ge(spread, h + 1)
                    over(dve, masked, h - 1)
                    over(dve, lasts, h - 1)
                    dve.tensor_scalar(cell.e[y][:, :], bank[4][:, 0:P], cols[:, PCH, 0, h:h + 1], 0.0, ALU.add,
                                      ALU.min).then_inc(exp_in, 1)
                    dve.tensor_copy(adec[:, h, :], bank[4][:, P:2 * P])
                    dve.wait_ge(projected, h + 1)
                    dve.tensor_copy(flat(v[h]), bank[3][:, :]).then_inc(vcopied, 1)
                    dve.wait_ge(qk, h + 1)
                    dve.tensor_tensor(qa[h][:, :, :], cell.q[y][:, :, :], bcast(bank[4][:, P:2 * P], 1, HT), ALU.mult).then_inc(d_bank4, 1)
                    dve.wait_ge(lasts, h + 1)
                    dve.tensor_reduce(wg[:, h:h + 1], cell.h[y][:, 0, :], AX.X, ALU.add).then_inc(summed, 1)
                    dve.wait_ge(masked, h + 1)
                    dve.wait_ge(scored, h + 1)
                    dve.tensor_tensor(sc[h][:, :], cell.em[y][:, :], bank[5][:, 0:P], ALU.mult).then_inc(weighted, 1)

        turned, copied, cut_out, added, updated, inter, kept, let = (env.sem(n) for n in (
            "turned", "copied", "cut_out", "added", "updated", "inter", "kept", "let"))
        c_kept = [env.sem(f"c_kept{k}") for k in range(2)]

        def streams(eng, body):
            for h in range(HEADS):
                for s in range(2):
                    body(h, s, s, STREAMS * h + s)
                with eng.Fori(1, STREAMS // 2) as k:
                    for p in range(2):
                        body(h, k * 2 + p, p, k * 2 + (STREAMS * h + p))

        with nc.Block() as block:
            @block.sync
            def _(sp):
                def store(p, s, h):
                    dst = c_out[0, s, h].rearrange("(t p) k -> p t k", p=P) if isinstance(s, int) else \
                        c_out[0, bass.ds(s, 1), h].rearrange("o (t p) k -> p (o t) k", p=P)
                    sp.dma_start(dst, cnew[p][:, :, :]).then_inc(c_kept[p], 16)

                def body(h, s, p, i):
                    if isinstance(i, int) and i < 2:
                        return
                    sp.wait_ge(updated, i * HT - HT)
                    if not isinstance(i, int):
                        held(sp, let)
                    c_load(sp, p, s, h)
                    store(p, *((s - 2, h) if not isinstance(s, int) else (STREAMS - 2 + s, h - 1)))

                streams(sp, body)
                for p in range(2):
                    sp.wait_ge(updated, HT * (SR - 1 + p))
                    store(p, STREAMS - 2 + p, HEADS - 1)
                for p in range(2):
                    sp.wait_ge(c_kept[p], 8 * SR)

            @block.tensor
            def _(pe):
                def body(h, s, p, i):
                    pe.wait_ge(c_in[p], i * 8 + (16 - 8 * p))
                    for k in range(HT):
                        if not isinstance(i, int) or i:
                            pe.wait_ge(copied, i * HT - (HT - 1 - k))
                        for t in range(HT):
                            ins = pe.transpose(bank[k][:, P * t:P * t + P], craw[p][:, t, P * k:P * k + P], env.ident[:, :])
                        ins.then_inc(turned, 1)
                    pe.wait_ge(cut_out, i + 1)
                    for t in range(HT):
                        over(pe, updated, i * HT + (t - 1))
                        pe.matmul(bank[5 + 2 * (t % 2)][:, :], v[h][:, t, :], flat(kwm[p]), start=True, stop=True).then_inc(added, 1)
                    pe.wait_ge(copied, i * HT + HT)
                    if isinstance(s, int) and s == 0:
                        over(pe, kept, h)
                    for t in range(HT):
                        for k in range(HT):
                            if isinstance(s, int):
                                out = bank[6][:, P * t + STEPS * s:P * t + STEPS * s + STEPS]
                                rhs = qa[h][:, k, STEPS * s:STEPS * s + STEPS]
                            else:
                                out, rhs = bank[6][:, bass.ds(s * STEPS + P * t, STEPS)], qa[h][:, k, bass.ds(s * STEPS, STEPS)]
                            ins = pe.matmul(out, cts[:, k, P * t:P * t + P], rhs, start=(k == 0), stop=(k == HT - 1))
                    ins.then_inc(inter, 1)
                streams(pe, body)

            @block.scalar
            def _(act):
                def body(h, s, p, i):
                    over(act, added, i * HT - HT)
                    act.activation(flat(kwm[p]), flat(kw[h]), ACT.Copy, scale=member[:, s:s + 1] if isinstance(s, int) else
                                   member[:, bass.ds(s, 1)]).then_inc(cut_out, 1)
                    for k in range(HT):
                        act.wait_ge(turned, i * HT + (k + 1))
                        if k == 0:
                            over(act, inter, i)
                        act.activation(cts[:, k, :], bank[k][:, :], ACT.Copy).then_inc(copied, 1)

                for h in range(HEADS):
                    for s in range(2):
                        body(h, s, s, STREAMS * h + s)
                    with act.Fori(1, STREAMS // 2) as k:
                        for p in range(2):
                            body(h, k * 2 + p, p, k * 2 + (STREAMS * h + p))
                    act.wait_ge(inter, STREAMS * h + STREAMS)
                    act.activation(flat(inter_t[h]), bank[6][:, :], ACT.Copy).then_inc(kept, 1)

            @block.vector
            def _(dve):
                def body(h, s, p, i):
                    if not isinstance(i, int) or i >= 2:
                        dve.wait_ge(c_kept[p], i * 8 - 8 * p)
                    dec = adec[:, h, STEPS * s + STEPS - 1:STEPS * s + STEPS] if isinstance(s, int) else \
                        adec[:, h, bass.ds(s * STEPS + (STEPS - 1), 1)]
                    for t in range(HT):
                        dve.wait_ge(added, i * HT + (t + 1))
                        dve.scalar_tensor_tensor(out=cnew[p][:, t, :], in0=craw[p][:, t, :], scalar=dec,
                                                 in1=bank[5 + 2 * (t % 2)][:, :], op0=ALU.mult, op1=ALU.add).then_inc(updated, 1)
                streams(dve, body)

        out = [bank[k] for k in (5, 7, 1, 2)]
        (weighed, dened, numbered, d_num, bounded, scale_in, n_scaled, n_done, n_rows, n_kept, n_out_s, rowed, stats_in, stat,
         aimed, powed, normed, turned2, joined, joined2, skipped, finished) = (env.sem(n) for n in (
             "weighed", "dened", "numbered", "d_num", "bounded", "scale_in", "n_scaled", "n_done", "n_rows", "n_kept",
             "n_out_s", "rowed", "stats_in", "stat", "aimed", "powed", "normed", "turned2", "joined", "joined2", "skipped",
             "finished"))
        y_in = [env.sem(f"y_in{k}") for k in range(2)]
        den, rec = wg, cell.mv[0]
        with nc.Block() as block:
            @block.sync
            def _(sp):
                for h in range(HEADS):
                    over(sp, finished, h - 1)
                    for dst, src in ((cell.xc, xc_d), (cell.sz, sz_d)):
                        sp.dma_start(dst[h % 2][:, :, :], src.rearrange("k p t -> p k t")[:, HT * h:HT * h + HT, last]).then_inc(
                            y_in[h % 2], 16)
                sp.wait_ge(n_kept, 1)
                for h in range(HEADS):
                    sp.dma_start(n_out[0, :, h, :], nrow[STREAMS * h:STREAMS * h + STREAMS, :]).then_inc(n_out_s, 16)
                sp.wait_ge(n_out_s, 16 * HEADS)

            @block.tensor
            def _(pe):
                for h in range(HEADS):
                    pe.wait_ge(weighed, h + 1)
                    pe.matmul(bank[4][:, 256 + h:257 + h], sc[h][:, :], env.ones[:, 0:1], start=True, stop=False)
                    for k in range(HT):
                        pe.matmul(bank[4][:, 256 + h:257 + h], craw[h % 2][:, k, P * (h // 2):P * (h // 2) + P],
                                  env.ones[:, 0:1], start=False, stop=(k == HT - 1))
                    for k in range(HT):
                        ins = pe.matmul(bank[4][:, SR * k + STREAMS * h:SR * k + STREAMS * h + STREAMS], kw[h][:, k, :],
                                        member[:, :], start=True, stop=True)
                ins.then_inc(dened, 1)
                for h in range(HEADS):
                    pe.matmul(out[h][:, :], sc[h][:, :], flat(v[h]), start=True, stop=False, skip_group_check=True)
                    for t in range(HT):
                        ins = pe.matmul(out[h][:, P * t:P * t + P], inter_t[h][:, t, :], env.ident[:, :], start=False,
                                        stop=(t == HT - 1), skip_group_check=True)
                    ins.then_inc(numbered, 1)
                pe.wait_ge(n_done, 1)
                for k in range(HT):
                    ins = pe.transpose(bank[0][0:SR, P * k:P * k + P], nn[:, k, :, :].rearrange("p h s -> p (h s)"), env.ident[:, :])
                ins.then_inc(n_rows, 1)
                for h in range(HEADS):
                    pe.wait_ge(normed, h + 1)
                    for t in range(HT):
                        ins = pe.transpose(out[h][:, P * t:P * t + P], cell.hn[h % 2][:, t, :], env.ident[:, :])
                    ins.then_inc(turned2, 1)

            @block.scalar
            def _(act):
                act.wait_ge(scale_in, 1)
                for h in range(HEADS):
                    act.wait_ge(numbered, h + 1)
                    over(act, normed, h - 1)
                    act.activation(flat(cell.h[h % 2]), out[h][:, :], ACT.Copy, scale=den[:, h:h + 1]).then_inc(rowed, 1)
                act.wait_ge(n_rows, 1)
                act.activation(nrow[:, :], bank[0][0:SR, :], ACT.Copy).then_inc(n_kept, 1)

            @block.gpsimd
            def _(pool):
                for h in range(HEADS):
                    y, tiles = h % 2, slice(HT * h, HT * h + HT)
                    pool.wait_ge(y_in[y], 32 * (h // 2 + 1))
                    over(pool, joined2, h - 1)
                    pool.tensor_tensor(cell.t2[y][:, :, :], cell.xc[y][:, :, :], bcast(par[:, tiles, M_SKIP], 2, P),
                                       ALU.mult).then_inc(skipped, 1)
                    pool.wait_ge(aimed, h + 1)
                    pool.tensor_tensor(cell.small[y][:, 2:3], cell.small[y][:, 3:4], env.minus_half[:, :], ALU.pow).then_inc(powed, 1)
                    pool.wait_ge(joined2, h + 1)
                    pool.tensor_tensor(hs[:, tiles, last], cell.t1[y][:, :, :], cell.sz[y][:, :, :], ALU.mult).then_inc(finished, 1)

            @block.vector
            def _(dve):
                n_view = nt[:, :, :].rearrange("p k (s h) -> p k s h", h=HEADS)
                for h in range(HEADS):
                    for k in range(HT):
                        ins = dve.tensor_tensor(by_stream(craw[h % 2][:, k, P * (h // 2):P * (h // 2) + P]), by_stream(qa[h][:, k, :]),
                                                bcast(n_view[:, k, :, h], 2, STEPS), ALU.mult)
                    ins.then_inc(weighed, 1)
                for k in range(HT):
                    ins = dve.tensor_tensor(nn[:, k, :, :], n_view[:, k, :, :].rearrange("p s h -> p h s"),
                                            adec[:, :, STEPS - 1::STEPS], ALU.mult)
                ins.then_inc(n_scaled, 1)
                dve.wait_ge(n_scaled, 1)
                dve.wait_ge(dened, 1)
                dve.tensor_tensor(den[:, :], bank[4][:, 256:256 + HEADS], cols[:, PCH, 1, :], ALU.max).then_inc(bounded, 1)
                dve.tensor_tensor(nn[:, :, :, :].rearrange("p k h s -> p (k h s)"), nn[:, :, :, :].rearrange("p k h s -> p (k h s)"),
                                  bank[4][:, 0:HT * SR], ALU.add).then_inc(n_done, 1)
                dve.wait_ge(bounded, 1)
                dve.scalar_tensor_tensor(out=den[:, :], in0=bank[4][:, 256:256 + HEADS], scalar=-1.0, in1=den[:, :], op0=ALU.mult,
                                         op1=ALU.max).then_inc(bounded, 1)
                dve.wait_ge(bounded, 2)
                dve.reciprocal(den[:, :], den[:, :]).then_inc(scale_in, 1)
                for h in range(HEADS):
                    y, tiles = h % 2, slice(HT * h, HT * h + HT)
                    dve.wait_ge(rowed, h + 1)
                    dve.bn_stats(cell.stats[y][:, :], flat(cell.h[y])).then_inc(stats_in, 1)
                    dve.wait_ge(stats_in, h + 1)
                    dve.bn_aggr(cell.mv[y][:, :], cell.stats[y][:, :]).then_inc(stat, 1)
                    dve.wait_ge(stat, h + 1)
                    dve.tensor_scalar(cell.small[y][:, 3:4], cell.mv[y][:, 1:2], LN_EPS, None, ALU.add).then_inc(aimed, 1)
                    dve.wait_ge(powed, h + 1)
                    over(dve, turned2, h - 1)
                    dve.tensor_scalar(flat(cell.hn[y]), flat(cell.h[y]), cell.mv[y][:, 0:1], cell.small[y][:, 2:3],
                                      ALU.subtract, ALU.mult).then_inc(normed, 1)
                    dve.wait_ge(turned2, h + 1)
                    over(dve, finished, h - 1)
                    dve.tensor_tensor(cell.t1[y][:, :, :], four(out[h][:, :]), bcast(par[:, tiles, M_GAIN], 2, P), ALU.mult).then_inc(joined, 1)
                    dve.wait_ge(joined, h + 1)
                    dve.wait_ge(skipped, h + 1)
                    dve.tensor_tensor(flat(cell.t1[y]), flat(cell.t1[y]), flat(cell.t2[y]), ALU.add).then_inc(joined2, 1)


def mlstm_down(env, w_down, hs, f):
    nc, w, banks = env.nc, env.w, [env.bank[0:NB], env.bank[NB:2 * NB]]
    n0 = env.units
    B = IT // 2
    env.units = n0 + 2 * B
    down_src = w_down[0].rearrange("(t p) m -> p t m", p=P)
    with ExitStack() as scope:
        env.scope = scope
        a_head = [env.sb(f"a_head{k}", [P, 2, T], F32R) for k in range(2)]
        a_rest = [env.sb(f"a_rest{k}", [P, 2, T], F32R) for k in range(2)]
        ready, headed, rested, down, added = (env.sem(n) for n in ("ready", "headed", "rested", "down", "added"))

        def blocks(eng, body):
            body(0, 0, n0, False)
            body(1, 1, n0 + 2, False)
            with eng.Fori(1, B // 2 - 1) as i:
                for p in range(2):
                    body(i * 2 + p, p, i * 4 + (n0 + 2 * p), False)
            for b in range(B - 2, B):
                body(b, b % 2, n0 + 2 * b, b == B - 1)

        def part(b):
            return hs[:, 2 * b:2 * b + 2, :] if isinstance(b, int) else hs[:, bass.ds(b * 2, 2), :]

        with nc.Block() as block:
            @block.sync
            def _(sp):
                def body(b, p, n, last):
                    for h in range(2):
                        rows = down_src[:, 2 * b:2 * b + 2, :] if isinstance(b, int) else down_src[:, bass.ds(b * 2, 2), :]
                        w.load(sp, n + h, h, rows[:, :, 4 * P * h:4 * P * h + 4 * P], first=isinstance(n, int) and n + h < 2)
                blocks(sp, body)

            @block.gpsimd
            def _(pool):
                pool.memset(f[:, :, :], 0.0).then_inc(ready, 1)

            @block.tensor
            def _(pe):
                def body(b, p, n, last):
                    pe.wait_ge(rested, b + 1)
                    for m in range(KD):
                        if m % 4 == 0:
                            w.ready(pe, n + m // 4)
                        if not isinstance(b, int) or 8 * b + m >= 2:
                            pe.wait_ge(added, b * 8 + (m - 1))
                        for k in range(2):
                            cols = slice(4 * P * k + P * (m % 4), 4 * P * k + P * (m % 4) + P)
                            for lhs, rhs, q in ((w.head, a_head, 0), (w.head, a_rest, 1), (w.rest, a_head, 2)):
                                for c in range(NB):
                                    ins = pe.matmul(banks[m % 2][c][:, 0:TB], lhs[m // 4][:, cols],
                                                    rhs[p][:, k, TB * c:TB * c + TB], start=(k == 0 and q == 0),
                                                    stop=(k == 1 and q == 2))
                        ins.then_inc(w.used if m % 4 == 3 else down, 1)
                blocks(pe, body)

            @block.scalar
            def _(act):
                def heads(b, p, n):
                    if not isinstance(b, int) or b >= 2:
                        act.wait_ge(w.used, n - 2)
                    act.activation(a_head[p][:, :, :], part(b), ACT.Copy).then_inc(headed, 1)

                w.round(act, n0, 0, first=(n0 == 0))
                w.round(act, n0 + 1, 1, first=(n0 == 0))
                heads(0, 0, n0)

                def body(b, p, n, last):
                    if not last:
                        heads(b + 1, 1 - p, n + 2)
                        for h in range(2):
                            w.round(act, n + (2 + h), h)
                blocks(act, body)

            @block.vector
            def _(dve):
                def rests(b, p):
                    dve.wait_ge(headed, b + 1)
                    dve.tensor_tensor(a_rest[p][:, :, :], part(b), a_head[p][:, :, :].bitcast(F32), ALU.subtract).then_inc(rested, 1)

                w.subtract(dve, n0, 0)
                w.subtract(dve, n0 + 1, 1)
                rests(0, 0)
                dve.wait_ge(ready, 1)

                def body(b, p, n, last):
                    if not last:
                        rests(b + 1, 1 - p)
                    for m in range(KD):
                        if m % 4 == 3:
                            dve.wait_ge(w.used, n + (m // 4 + 1))
                        else:
                            dve.wait_ge(down, b * 6 + (m + 1 - m // 4))
                        for c in range(NB):
                            ins = dve.tensor_tensor(f[:, m, TB * c:TB * c + TB], f[:, m, TB * c:TB * c + TB],
                                                    banks[m % 2][c][:, 0:TB], ALU.add)
                        ins.then_inc(added, 1)
                        if m % 4 == 3 and not last:
                            w.subtract(dve, n + (2 + m // 4), m // 4)
                blocks(dve, body)


def rows_back(env, x_dram, y_prompt, y_sample):
    nc, bank = env.nc, env.bank
    R = T // P
    with ExitStack() as scope:
        env.scope = scope
        xt = [env.sb(f"xt{k}", [P, KD, P]) for k in range(2)]
        xr = [env.sb(f"xr{k}", [P, D]) for k in range(2)]
        x_in = [env.sem(f"x_in{k}") for k in range(2)]
        kept = [env.sem(f"kept{k}") for k in range(2)]
        turned, copied = env.sem("turned"), env.sem("copied")
        yp, ys = y_prompt[0], y_sample.rearrange("s j d -> (s j) d")
        with nc.Block() as block:
            @block.sync
            def _(sp):
                for r in range(R):
                    if r >= 2:
                        sp.wait_ge(turned, 2 * (r - 1))
                    sp.dma_start(xt[r % 2][:, :, :], x_dram.rearrange("k p t -> p k t")[:, :, P * r:P * r + P]).then_inc(x_in[r % 2], 16)

            @block.tensor
            def _(pe):
                for r in range(R):
                    pe.wait_ge(x_in[r % 2], 16 * (r // 2 + 1))
                    for h in range(2):
                        if r >= 4:
                            pe.wait_ge(copied, 2 * (r - 4) + h + 1)
                        for q in range(4):
                            m = pe.transpose(bank[2 * (r % 4) + h][:, P * q:P * q + P], xt[r % 2][:, 4 * h + q, :], env.ident[:, :])
                        m.then_inc(turned, 1)

            @block.scalar
            def _(act):
                for r in range(R):
                    if r >= 2:
                        act.wait_ge(kept[r % 2], 16 * (r // 2))
                    for h in range(2):
                        act.wait_ge(turned, 2 * r + h + 1)
                        act.activation(xr[r % 2][:, 512 * h:512 * h + 512], bank[2 * (r % 4) + h][:, :], ACT.Copy).then_inc(copied, 1)

            @block.gpsimd
            def _(pool):
                for r in range(R):
                    pool.wait_ge(copied, 2 * r + 2)
                    pool.dma_start(yp[P * r:P * r + P, :] if r < SEQ // P else ys, xr[r % 2][:, :]).then_inc(kept[r % 2], 16)
                for k in range(2):
                    pool.wait_ge(kept[k], 16 * ((R + 1 - k) // 2))


def program(nc, i, o):
    (y_prompt, y_sample, p_re, p_im, p_c, p_n, p_m, p_mconv, p_fconv,
     s_re, s_im, s_c, s_n, s_m, s_mconv, s_fconv) = o
    with ExitStack() as outer:
        env = Env(nc, outer)
        env.bank = [outer.enter_context(nc.psum_tensor(f"bank{k}", [P, 512], F32)) for k in range(8)]
        constants(env)
        env.gains = env.sb("gains", [P, KD, 8])
        gains_in(env, i["norm_g"])
        z_rows, x_res = env.dram("z_rows", [T, D]), env.dram("x_res", [KD, P, T])
        xm_d, xc_d, sz_d = (env.dram(n, [IT, P, T]) for n in ("xm_d", "xc_d", "sz_d"))

        s5(env, i, z_rows, [p_re, p_im, s_re, s_im])

        def conv_ffn(layer, base, x_head, x_rest, f):
            with ExitStack() as scope:
                env.scope = scope
                par = env.sb("par", [P, 2 * FT, STREAMS * (FTAPS - 1) + FTAPS + 1])
                tails = env.sb("tails", [P, 2 * FT, (STREAMS + 1) * (FTAPS - 1)])
                params_in(env, par, [i["state_ffn_conv"][layer].rearrange("s h m -> (s h) m"), i["ffn_conv_w"][layer],
                                     i["ffn_conv_b"][layer:layer + 1, :]], 2 * FT, STREAMS * (FTAPS - 1) + FTAPS + 1)
                ffn(env, i["ffn_w_up"][layer], i["ffn_w_down"][layer], par, tails, x_head, x_rest, f)
                rows_out(env, tails, [(s_fconv[layer].rearrange("s h m -> (s h) m"), 0),
                                      (p_fconv[layer, 0], STREAMS * (FTAPS - 1))], 2 * FT, (STREAMS + 1) * (FTAPS - 1))

        mixer = outer.enter_context(ExitStack())
        with ExitStack() as scope:
            env.scope = mixer
            par = env.sb("m_par", [P, IT, M_ROWS])
            gates = env.sb("gates", [2 * HEADS, T])
            env.scope, env.units = scope, 0
            env.w = Weights(env)
            x_head, x_rest = env.sb("x_head", [P, KD, T], F32R), env.sb("x_rest", [P, KD, T], F32R)
            with ExitStack() as inner:
                env.scope = inner
                f = env.sb("f", [P, KD, T])
                rows_in(env, z_rows, i["x_prompt"], i["x_sample"], x_res, x_head, x_rest)
                glu(env, i["s5_w_glu"], x_head, x_rest, f)
                norm_add_norm(env, f, x_res, 1, 2, x_head, x_rest)
                conv_ffn(0, inner, x_head, x_rest, f)
                norm_add_norm(env, f, x_res, 3, 4, x_head, x_rest)
            params_in(env, par, [i["state_mlstm_conv"][0].rearrange("s h m -> (s h) m"), i["mlstm_conv_w"][0],
                                 i["mlstm_conv_b"][0:1, :], i["mlstm_norm_g"][0:1, :], i["mlstm_skip"][0:1, :]], IT, M_ROWS)
            with ExitStack() as inner:
                env.scope = inner
                tails, gate_w = env.sb("m_tails", [P, IT, (STREAMS + 1) * MH]), env.sb("gate_w", [P, IT, 4 * HEADS])
                with ExitStack() as brief:
                    env.scope = brief
                    headwise_weights(env, i["mlstm_wq"], i["mlstm_wk"], i["mlstm_wv"], i["mlstm_w_gate"],
                                     env.sb("bd", [P, 3, IT, P]), gate_w)
                mlstm_up(env, i["mlstm_w_up"], par, tails, gate_w, i["mlstm_b_gate"], x_head, x_rest, xm_d, xc_d, sz_d, gates)
                rows_out(env, tails, [(s_mconv[0].rearrange("s h m -> (s h) m"), 0), (p_mconv[0, 0], STREAMS * MH)],
                         IT, (STREAMS + 1) * MH)
        env.new_phase()
        env.scope = mixer
        f = env.sb("f", [P, KD, T])
        passed = outer.enter_context(ExitStack())
        env.scope = passed
        hs = env.sb("hs", [P, IT, T])
        with ExitStack() as scope:
            env.scope = scope
            bd = env.sb("bd", [P, 3, IT, P])
            with ExitStack() as brief:
                env.scope = brief
                headwise_weights(env, i["mlstm_wq"], i["mlstm_wk"], i["mlstm_wv"], i["mlstm_w_gate"], bd,
                                 env.sb("gate_w", [P, IT, 4 * HEADS]))
            env.scope = scope
            rows, cols = env.sb("rows", [HEADS, CHUNKS, 2, P]), env.sb("cols", [P, CHUNKS, 2, HEADS])
            gate_rows(env, gates, i["state_mlstm_m"], rows, cols, p_m, s_m)
            env.scope = scope
            tri, tri_s, last_s = (env.sb(n, [P, P]) for n in ("tri", "tri_s", "last_s"))
            member = env.sb("member", [P, STREAMS])
            cell_masks(env, tri, tri_s, last_s, member)
            cell = Cell(env, bd)
            mlstm_prompt(env, cell, par, rows, cols, tri, xm_d, xc_d, sz_d, hs, f, p_c, p_n)
            mlstm_streams(env, cell, par, rows, cols, tri_s, last_s, member, xm_d, xc_d, sz_d, i["state_mlstm_C"],
                          i["state_mlstm_n"], hs, f, s_c, s_n)
        env.new_phase()
        env.scope, env.units = passed, 0
        env.w = Weights(env)
        mlstm_down(env, i["mlstm_w_down"], hs, f)
        passed.close()
        env.scope, env.units = mixer, 0
        env.w = Weights(env)
        x_head, x_rest = env.sb("x_head", [P, KD, T], F32R), env.sb("x_rest", [P, KD, T], F32R)
        norm_add_norm(env, f, x_res, 5, 6, x_head, x_rest)
        conv_ffn(1, None, x_head, x_rest, f)
        norm_add_norm(env, f, x_res, 7, None, y=x_res)
        rows_back(env, x_res, y_prompt, y_sample)


_INS = [
    "x_prompt", "x_sample", "state_s5_re", "state_s5_im", "state_mlstm_C", "state_mlstm_n",
    "state_mlstm_m", "state_mlstm_conv", "state_ffn_conv", "norm_g", "s5_A_re", "s5_A_im",
    "s5_log_dt", "s5_B_re", "s5_B_im", "s5_C_re", "s5_C_im", "s5_D",
    "s5_w_glu", "mlstm_w_up", "mlstm_conv_w", "mlstm_conv_b", "mlstm_wq", "mlstm_wk",
    "mlstm_wv", "mlstm_w_gate", "mlstm_b_gate", "mlstm_norm_g", "mlstm_skip", "mlstm_w_down",
    "ffn_w_up", "ffn_conv_w", "ffn_conv_b", "ffn_w_down",
]
_OUTS = [
    (1, 1024, 1024),
    (8, 16, 1024),
    (1, 1, 64, 64),
    (1, 1, 64, 64),
    (1, 1, 4, 512, 512),
    (1, 1, 4, 512),
    (1, 1, 4),
    (1, 1, 3, 2048),
    (2, 1, 2, 5632),
    (1, 8, 64, 64),
    (1, 8, 64, 64),
    (1, 8, 4, 512, 512),
    (1, 8, 4, 512),
    (1, 8, 4),
    (1, 8, 3, 2048),
    (2, 8, 2, 5632),
]


def kernel(**inputs):
    import numpy as _np
    import concourse.bacc as _bacc
    from concourse import mybir as _mybir
    from concourse.bass_utils import run_bass_kernel_spmd as _run

    nc = _bacc.Bacc("TRN2", target_bir_lowering=False, num_devices=1)
    arrays, ins, outs = {}, {}, []
    for name in _INS:
        a = _np.ascontiguousarray(inputs[name])
        arrays[f"in_{name}_dram"] = a
        ins[name] = nc.dram_tensor(f"in_{name}_dram", a.shape, _mybir.dt.from_np(a.dtype), kind="ExternalInput").ap()
    for i, shape in enumerate(_OUTS):
        outs.append(nc.dram_tensor(f"out_{i}_dram", shape, _mybir.dt.float32, kind="ExternalOutput").ap())
    program(nc, ins, outs)
    r = _run(nc, [arrays], core_ids=[0])
    return tuple(r.results[0][f"out_{i}_dram"] for i in range(len(_OUTS)))
```
